# Optimizing a Trainium2 kernel written in Bass

```python
import jax, jax.numpy as jnp
from jax import lax
import numpy as np

D_MODEL = 1024
BATCH = 1
SEQ = 256
DEPTH = 2

CHUNK = 64
N_A_LAYERS = DEPTH // 2
N_B_LAYERS = DEPTH - N_A_LAYERS
MIX_WIDTH = D_MODEL
MEM_TOKENS = 256
MEM_HEADS = 4
MEM_WIDTH = D_MODEL // 4
MEM_HEAD_DIM = MEM_WIDTH // MEM_HEADS
A_WIDTH = MIX_WIDTH - MEM_WIDTH
A_HEADS = 4
A_HEAD_DIM = A_WIDTH // A_HEADS
A_CONV = 4
B_HEAD_DIM = 64
B_HEADS = A_WIDTH // B_HEAD_DIM
B_WIDTH = B_HEADS * B_HEAD_DIM
BAND_CHUNKS = 9
BAND = BAND_CHUNKS * CHUNK
KV_PAD = BAND - CHUNK
MAX_REL = 128
REL_SIZE = MAX_REL + CHUNK
D_FF = ((8 * D_MODEL // 3 + 127) // 128) * 128
FFN_CONV = 3
A_IN = 4 * A_WIDTH + 2 * A_HEADS + MEM_WIDTH
B_IN = B_WIDTH + MEM_WIDTH
EPS = 1e-6


def rmsnorm(x, g):
    x32 = x.astype(jnp.float32)
    y = x32 * lax.rsqrt(jnp.mean(x32 * x32, axis=-1, keepdims=True) + EPS)
    return (y * g.astype(jnp.float32)).astype(x.dtype)

def causal_dwconv(x, w, b):
    k = w.shape[0]
    s = x.shape[1]
    xp = jnp.pad(x, ((0, 0), (k - 1, 0), (0, 0)))
    y = xp[:, 0:s] * w[0]
    for j in range(1, k):
        y = y + xp[:, j:j + s] * w[j]
    return y + b

def mlstm_chunkwise(q, k, v, ig, logf):
    bsz, seq, nh, dh = q.shape
    nc = seq // CHUNK
    f32 = jnp.float32

    def to_chunks(t):
        t = t.astype(f32).reshape((bsz, nc, CHUNK) + t.shape[2:])
        perm = (1, 0, 3, 2) + tuple(range(4, t.ndim))
        return t.transpose(perm)

    qc, kc, vc = to_chunks(q), to_chunks(k * (dh ** -0.5)), to_chunks(v)
    igc, lfc = to_chunks(ig), to_chunks(logf)
    tril = jnp.tril(jnp.ones((CHUNK, CHUNK), dtype=bool))

    def step(carry, inp):
        c_st, n_st, m_st = carry
        qq, kk, vv, ii, lf = inp
        b = jnp.cumsum(lf, axis=-1)
        d = b[..., :, None] - b[..., None, :] + ii[..., None, :]
        d = jnp.where(tril, d, -jnp.inf)
        m_inter = b + m_st[..., None]
        m_t = jnp.maximum(m_inter, jnp.max(d, axis=-1))
        inter = jnp.exp(m_inter - m_t)
        s = jnp.einsum('bhtd,bhsd->bhts', qq, kk) * jnp.exp(d - m_t[..., None])
        num = jnp.einsum('bhts,bhse->bhte', s, vv) + inter[..., None] * jnp.einsum('bhtd,bhde->bhte', qq, c_st)
        den = jnp.sum(s, axis=-1) + inter * jnp.einsum('bhtd,bhd->bht', qq, n_st)
        h = num / jnp.maximum(jnp.abs(den), jnp.exp(-m_t))[..., None]
        b_last = b[..., -1]
        w = b_last[..., None] - b + ii
        m_new = jnp.maximum(b_last + m_st, jnp.max(w, axis=-1))
        w_exp = jnp.exp(w - m_new[..., None])
        decay = jnp.exp(b_last + m_st - m_new)
        c_new = decay[..., None, None] * c_st + jnp.einsum('bhs,bhsd,bhse->bhde', w_exp, kk, vv)
        n_new = decay[..., None] * n_st + jnp.einsum('bhs,bhsd->bhd', w_exp, kk)
        return (c_new, n_new, m_new), h

    init = (jnp.zeros((bsz, nh, dh, dh), f32), jnp.zeros((bsz, nh, dh), f32), jnp.zeros((bsz, nh), f32))
    _, h = lax.scan(step, init, (qc, kc, vc, igc, lfc))
    return h.transpose(1, 0, 3, 2, 4).reshape(bsz, seq, nh, dh)

def band_attention(q, k_pad, v_pad, rel_table):
    bsz, seq, _ = q.shape
    nc = seq // CHUNK
    q = q.reshape(bsz, seq, B_HEADS, B_HEAD_DIM)
    qi = jnp.arange(CHUNK)
    kj = jnp.arange(BAND)
    rel = KV_PAD + qi[:, None] - kj[None, :]
    idx = jnp.clip(rel, -(CHUNK - 1), MAX_REL) + (CHUNK - 1)
    bias = rel_table.astype(jnp.float32)[:, idx]
    scale = B_HEAD_DIM ** -0.5

    def one_chunk(c):
        start = c * CHUNK
        qc = lax.dynamic_slice_in_dim(q, start, CHUNK, axis=1)
        kc = lax.dynamic_slice_in_dim(k_pad, start, BAND, axis=1)
        vc = lax.dynamic_slice_in_dim(v_pad, start, BAND, axis=1)
        s = jnp.einsum('bqhd,bkhd->bhqk', qc, kc).astype(jnp.float32) * scale + bias
        valid = (start - KV_PAD + kj) >= 0
        s = jnp.where(valid, s, -jnp.inf)
        p = jax.nn.softmax(s, axis=-1).astype(vc.dtype)
        return jnp.einsum('bhqk,bkhd->bqhd', p, vc)

    out = lax.map(one_chunk, jnp.arange(nc))
    return out.transpose(1, 0, 2, 3, 4).reshape(bsz, seq, B_WIDTH)

def memory_attention(q, mem, w_kv):
    bsz, seq, _ = q.shape
    q = q.reshape(bsz, seq, MEM_HEADS, MEM_HEAD_DIM)
    mk, mv = jnp.split(mem @ w_kv, 2, axis=-1)
    mk = mk.reshape(bsz, -1, MEM_HEADS, MEM_HEAD_DIM)
    mv = mv.reshape(bsz, -1, MEM_HEADS, MEM_HEAD_DIM)
    s = jnp.einsum('bshd,bmhd->bhsm', q, mk).astype(jnp.float32) * (MEM_HEAD_DIM ** -0.5)
    p = jax.nn.softmax(s, axis=-1).astype(mv.dtype)
    return jnp.einsum('bhsm,bmhd->bshd', p, mv).reshape(bsz, seq, MEM_WIDTH)

def conv_ffn(h, w_up, conv_w, conv_b, w_down):
    u, g = jnp.split(h @ w_up, 2, axis=-1)
    g = causal_dwconv(g, conv_w, conv_b)
    return (jax.nn.silu(g) * u) @ w_down

def first_inputs(seed: int = 0) -> dict:
    key = jax.random.key(seed)
    ks = jax.random.split(key, 24)
    f32 = jnp.float32

    def nrm(k, shape, scale):
        return jax.random.normal(k, shape, f32) * scale

    gate_b = jnp.concatenate([
        nrm(ks[5], (N_A_LAYERS, A_HEADS), 0.1),
        jnp.linspace(3.0, 6.0, A_HEADS, dtype=f32)[None, :] + nrm(ks[6], (N_A_LAYERS, A_HEADS), 0.1),
    ], axis=-1)
    return {
        "x": nrm(ks[0], (BATCH, SEQ, D_MODEL), 1.0),
        "mem": nrm(ks[1], (BATCH, MEM_TOKENS, D_MODEL), 1.0),
        "norm_mix_g": 1.0 + nrm(ks[2], (DEPTH, D_MODEL), 0.1),
        "norm_ffn_g": 1.0 + nrm(ks[3], (DEPTH, D_MODEL), 0.1),
        "a_w_in": nrm(ks[4], (N_A_LAYERS, D_MODEL, A_IN), D_MODEL ** -0.5),
        "a_gate_b": gate_b,
        "a_conv_w": nrm(ks[7], (N_A_LAYERS, A_CONV, 2 * A_WIDTH), A_CONV ** -0.5),
        "a_conv_b": nrm(ks[8], (N_A_LAYERS, 2 * A_WIDTH), 0.02),
        "a_head_g": 1.0 + nrm(ks[9], (N_A_LAYERS, A_WIDTH), 0.1),
        "a_w_out": nrm(ks[10], (N_A_LAYERS, MIX_WIDTH, D_MODEL), MIX_WIDTH ** -0.5),
        "kv_norm_g": 1.0 + nrm(ks[11], (D_MODEL,), 0.1),
        "w_kv": nrm(ks[12], (D_MODEL, 2 * B_WIDTH), D_MODEL ** -0.5),
        "b_w_in": nrm(ks[13], (N_B_LAYERS, D_MODEL, B_IN), D_MODEL ** -0.5),
        "b_rel_bias": nrm(ks[14], (N_B_LAYERS, B_HEADS, REL_SIZE), 0.5),
        "b_w_out": nrm(ks[15], (N_B_LAYERS, MIX_WIDTH, D_MODEL), MIX_WIDTH ** -0.5),
        "mem_w_kv": nrm(ks[16], (DEPTH, D_MODEL, 2 * MEM_WIDTH), D_MODEL ** -0.5),
        "ffn_w_up": nrm(ks[17], (DEPTH, D_MODEL, 2 * D_FF), D_MODEL ** -0.5),
        "ffn_conv_w": nrm(ks[18], (DEPTH, FFN_CONV, D_FF), FFN_CONV ** -0.5),
        "ffn_conv_b": nrm(ks[19], (DEPTH, D_FF), 0.02),
        "ffn_w_down": nrm(ks[20], (DEPTH, D_FF, D_MODEL), D_FF ** -0.5),
        "final_g": 1.0 + nrm(ks[21], (D_MODEL,), 0.1),
    }

def first_block(x, mem, norm_mix_g, norm_ffn_g, a_w_in, a_gate_b, a_conv_w, a_conv_b, a_head_g, a_w_out,
              kv_norm_g, w_kv, b_w_in, b_rel_bias, b_w_out, mem_w_kv, ffn_w_up, ffn_conv_w, ffn_conv_b,
              ffn_w_down, final_g):
    bsz, seq, _ = x.shape
    k_pad = None
    v_pad = None
    for l in range(DEPTH):
        h = rmsnorm(x, norm_mix_g[l])
        if l < N_A_LAYERS:
            a = l
            proj = h @ a_w_in[a]
            qk, v, o, gates, q_mem = jnp.split(
                proj, [2 * A_WIDTH, 3 * A_WIDTH, 4 * A_WIDTH, 4 * A_WIDTH + 2 * A_HEADS], axis=-1)
            qk = jax.nn.silu(causal_dwconv(qk, a_conv_w[a], a_conv_b[a]))
            q, k = jnp.split(qk, 2, axis=-1)
            gates = gates.astype(jnp.float32) + a_gate_b[a].astype(jnp.float32)
            ig, fg = jnp.split(gates, 2, axis=-1)
            hm = mlstm_chunkwise(q.reshape(bsz, seq, A_HEADS, A_HEAD_DIM),
                                 k.reshape(bsz, seq, A_HEADS, A_HEAD_DIM),
                                 v.reshape(bsz, seq, A_HEADS, A_HEAD_DIM),
                                 ig, jax.nn.log_sigmoid(fg))
            hm = hm * lax.rsqrt(jnp.mean(hm * hm, axis=-1, keepdims=True) + EPS)
            hm = hm.reshape(bsz, seq, A_WIDTH) * a_head_g[a].astype(jnp.float32)
            mix_out = (hm * jax.nn.sigmoid(o.astype(jnp.float32))).astype(x.dtype)
            w_out = a_w_out[a]
        else:
            bl = l - N_A_LAYERS
            proj = h @ b_w_in[bl]
            q, q_mem = jnp.split(proj, [B_WIDTH], axis=-1)
            mix_out = band_attention(q, k_pad, v_pad, b_rel_bias[bl])
            w_out = b_w_out[bl]
        mem_out = memory_attention(q_mem, mem, mem_w_kv[l])
        x = x + jnp.concatenate([mix_out, mem_out], axis=-1) @ w_out
        x = x + conv_ffn(rmsnorm(x, norm_ffn_g[l]), ffn_w_up[l], ffn_conv_w[l], ffn_conv_b[l], ffn_w_down[l])
        if l == N_A_LAYERS - 1:
            ks_, vs_ = jnp.split(rmsnorm(x, kv_norm_g) @ w_kv, 2, axis=-1)
            pad = ((0, 0), (KV_PAD, 0), (0, 0), (0, 0))
            k_pad = jnp.pad(ks_.reshape(bsz, seq, B_HEADS, B_HEAD_DIM), pad)
            v_pad = jnp.pad(vs_.reshape(bsz, seq, B_HEADS, B_HEAD_DIM), pad)
    return rmsnorm(x, final_g)


GRID_W = 64
CTX_LEN = 256

NA_HEADS = 8
NA_HEAD_DIM = 64
NA_WIDTH = NA_HEADS * NA_HEAD_DIM
NA_KH = 8
NA_KW = 16

HG_HEADS = 4
HG_KEY_DIM = 128
HG_VAL_DIM = 128
HG_KEY = HG_HEADS * HG_KEY_DIM
HG_VAL = HG_HEADS * HG_VAL_DIM
HG_CHUNK = 32

D_FF_2 = 2816
CONV_W = 3

N_EVEN = (DEPTH + 1) // 2
N_ODD = DEPTH // 2
EV_SIZES = [NA_WIDTH, NA_WIDTH, NA_WIDTH, HG_KEY, HG_KEY, HG_KEY, HG_VAL, HG_VAL]
EV_IN = sum(EV_SIZES)
EV_SPLITS = [int(s) for s in np.cumsum(EV_SIZES)[:-1]]
EV_MIX = NA_WIDTH + HG_VAL


def rms_norm(x, w):
    xf = x.astype(jnp.float32)
    y = xf * lax.rsqrt(jnp.mean(xf * xf, axis=-1, keepdims=True) + EPS)
    return (y * w.astype(jnp.float32)).astype(x.dtype)

def modulate(h, shift, scale):
    return h * (1.0 + scale[:, None, :]) + shift[:, None, :]

def dwconv3(h, w, b):
    hp = jnp.pad(h, ((0, 0), (1, 1), (0, 0)))
    return hp[:, :-2] * w[0] + hp[:, 1:-1] * w[1] + hp[:, 2:] * w[2] + b

def neighbourhood_attention(q, k, v, k_ctx, v_ctx, rpb):
    b, s, h, d = q.shape
    rows = s // GRID_W
    kh = min(NA_KH, rows)
    kw = NA_KW
    scale = d ** -0.5
    cols = np.arange(GRID_W)
    col_start = np.clip(cols - kw // 2, 0, GRID_W - kw)
    col_idx = col_start[:, None] + np.arange(kw)[None, :]
    col_rel = col_idx - cols[:, None] + (NA_KW - 1)
    rpb_c = rpb.astype(jnp.float32)[:, :, col_rel]
    qg = q.reshape(b, rows, GRID_W, h, d)
    kg = k.reshape(b, rows, GRID_W, h, d)
    vg = v.reshape(b, rows, GRID_W, h, d)

    def row_block(args):
        r, q_row = args
        r0 = jnp.clip(r - kh // 2, 0, rows - kh)
        k_rows = lax.dynamic_slice_in_dim(kg, r0, kh, axis=1)
        v_rows = lax.dynamic_slice_in_dim(vg, r0, kh, axis=1)
        k_nb = k_rows[:, :, col_idx]
        v_nb = v_rows[:, :, col_idx]
        row_rel = r0 + jnp.arange(kh) - r + (NA_KH - 1)
        bias = rpb_c[:, row_rel].transpose(0, 2, 1, 3)
        s_loc = jnp.einsum('bqhd,brqwhd->bhqrw', q_row, k_nb).astype(jnp.float32) * scale + bias[None]
        s_ctx = jnp.einsum('bqhd,bkhd->bhqk', q_row, k_ctx).astype(jnp.float32) * scale
        logits = jnp.concatenate([s_loc.reshape(b, h, GRID_W, kh * kw), s_ctx], axis=-1)
        p = jax.nn.softmax(logits, axis=-1).astype(v.dtype)
        p_loc = p[..., :kh * kw].reshape(b, h, GRID_W, kh, kw)
        p_ctx = p[..., kh * kw:]
        return (jnp.einsum('bhqrw,brqwhd->bqhd', p_loc, v_nb)
                + jnp.einsum('bhqk,bkhd->bqhd', p_ctx, v_ctx))

    out = lax.map(row_block, (jnp.arange(rows), qg.transpose(1, 0, 2, 3, 4)))
    return out.transpose(1, 0, 2, 3, 4).reshape(b, s, h, d)

def context_attention(q, k, v):
    s = jnp.einsum('bqhd,bkhd->bhqk', q, k).astype(jnp.float32) * (q.shape[-1] ** -0.5)
    p = jax.nn.softmax(s, axis=-1).astype(v.dtype)
    return jnp.einsum('bhqk,bkhd->bqhd', p, v)

def hgrn2_scan(q, k, v, log_f, s0):
    b, h, l, _ = q.shape
    n = l // HG_CHUNK

    def to_chunks(t):
        return t.reshape(b, h, n, HG_CHUNK, t.shape[-1]).transpose(2, 0, 1, 3, 4)

    causal_in_chunk = jnp.tril(jnp.ones((HG_CHUNK, HG_CHUNK), dtype=bool))

    def step(state, inp):
        qc, kc, vc, gc = inp
        bcum = jnp.cumsum(gc, axis=2)
        btot = bcum[:, :, -1:]
        qe = qc * jnp.exp(bcum)
        ke = kc * jnp.exp(-bcum)
        att = jnp.where(causal_in_chunk, jnp.einsum('bhtk,bhsk->bhts', qe, ke), 0.0)
        o = jnp.einsum('bhtk,bhkv->bhtv', qe, state) + jnp.einsum('bhts,bhsv->bhtv', att, vc)
        kd = kc * jnp.exp(btot - bcum)
        new_state = jnp.exp(btot)[:, :, 0, :, None] * state + jnp.einsum('bhsk,bhsv->bhkv', kd, vc)
        return new_state, o

    s_end, o = lax.scan(step, s0, (to_chunks(q), to_chunks(k), to_chunks(v), to_chunks(log_f)))
    return o.transpose(1, 2, 0, 3, 4).reshape(b, h, l, v.shape[-1]), s_end

def hgrn2_final_state(k, v, log_f):
    bcum = jnp.cumsum(log_f, axis=2)
    return jnp.einsum('bhtk,bhtv->bhkv', k * jnp.exp(bcum[:, :, -1:] - bcum), v)

def _heads(a, dh):
    b, l, _ = a.shape
    return a.astype(jnp.float32).reshape(b, l, -1, dh).transpose(0, 2, 1, 3)

def _hg_gates(f_pres, i, lb):
    v = _heads(i, HG_VAL_DIM)
    dirs = []
    for d, f_pre in enumerate(f_pres):
        lbd = lb[d].astype(jnp.float32).reshape(HG_HEADS, 1, HG_KEY_DIM)
        fg = lbd + (1.0 - lbd) * jax.nn.sigmoid(_heads(f_pre, HG_KEY_DIM))
        dirs.append((1.0 - fg, jnp.log(fg)))
    return v, dirs

def _hg_readout(o, g, norm_w):
    b, _, l, _ = o.shape
    o = o * lax.rsqrt(jnp.mean(o * o, axis=-1, keepdims=True) + EPS)
    o = o * norm_w.astype(jnp.float32).reshape(HG_HEADS, 1, HG_VAL_DIM)
    o = o.transpose(0, 2, 1, 3).reshape(b, l, HG_VAL)
    return (o * jax.nn.silu(g.astype(jnp.float32))).astype(g.dtype)

def hgrn2_mixer(q, fs, i, g, cq, cfs, ci, cg, lb, norm_w, with_ctx_out):
    v, dirs = _hg_gates(fs, i, lb)
    vc, dirs_c = _hg_gates(cfs, ci, lb)
    qh = jax.nn.silu(_heads(q, HG_KEY_DIM))
    if with_ctx_out:
        cqh = jax.nn.silu(_heads(cq, HG_KEY_DIM))
    b = q.shape[0]
    zero_state = jnp.zeros((b, HG_HEADS, HG_KEY_DIM, HG_VAL_DIM), jnp.float32)
    o_lat = jnp.zeros_like(qh[..., :HG_VAL_DIM])
    o_ctx = None
    for d in range(2):
        tr = (lambda a: jnp.flip(a, axis=2)) if d == 1 else (lambda a: a)
        k, lf = dirs[d]
        kc, lfc = dirs_c[d]
        if with_ctx_out:
            oc, s_ctx = hgrn2_scan(tr(cqh), tr(kc), tr(vc), tr(lfc), zero_state)
            o_ctx = tr(oc) if o_ctx is None else o_ctx + tr(oc)
        else:
            s_ctx = hgrn2_final_state(tr(kc), tr(vc), tr(lfc))
        ol, _ = hgrn2_scan(tr(qh), tr(k), tr(v), tr(lf), s_ctx)
        o_lat = o_lat + tr(ol)
    y = _hg_readout(o_lat, g, norm_w)
    y_ctx = _hg_readout(o_ctx, cg, norm_w) if with_ctx_out else None
    return y, y_ctx

def even_mixer(h, h_ctx, w_in, w_out, rpb, lb, hg_norm_w, with_ctx_out):
    b, s, _ = h.shape
    na_q, na_k, na_v, hg_q, hg_ff, hg_fb, hg_i, hg_g = jnp.split(h @ w_in, EV_SPLITS, axis=-1)
    cna_q, cna_k, cna_v, chg_q, chg_ff, chg_fb, chg_i, chg_g = jnp.split(h_ctx @ w_in, EV_SPLITS, axis=-1)

    def nh(a):
        return a.reshape(a.shape[0], a.shape[1], NA_HEADS, NA_HEAD_DIM)

    a_lat = neighbourhood_attention(nh(na_q), nh(na_k), nh(na_v), nh(cna_k), nh(cna_v), rpb)
    g_lat, g_ctx = hgrn2_mixer(hg_q, (hg_ff, hg_fb), hg_i, hg_g,
                               chg_q, (chg_ff, chg_fb), chg_i, chg_g, lb, hg_norm_w, with_ctx_out)
    y = jnp.concatenate([a_lat.reshape(b, s, NA_WIDTH), g_lat], axis=-1) @ w_out
    y_ctx = None
    if with_ctx_out:
        a_ctx = context_attention(nh(cna_q), nh(cna_k), nh(cna_v))
        y_ctx = jnp.concatenate([a_ctx.reshape(b, h_ctx.shape[1], NA_WIDTH), g_ctx], axis=-1) @ w_out
    return y, y_ctx

def short_conv_mixer(h, w_in, conv_w, conv_b, w_out):
    gate_b, gate_c, u = jnp.split(h @ w_in, 3, axis=-1)
    return (gate_b * dwconv3(gate_c * u, conv_w, conv_b)) @ w_out

def conv_ffn_2(h, w_up, conv_w, conv_b, w_down):
    a, val = jnp.split(h @ w_up, 2, axis=-1)
    return (jax.nn.gelu(dwconv3(a, conv_w, conv_b), approximate=False) * val) @ w_down

def second_inputs(seed: int = 0) -> dict:
    key = jax.random.key(seed)
    ks = jax.random.split(key, 24)
    f32 = jnp.float32
    nrm = lambda k, shape, s: jax.random.normal(k, shape, f32) * s
    D = D_MODEL
    return {
        "x": nrm(ks[0], (BATCH, SEQ, D), 1.0),
        "c": nrm(ks[1], (BATCH, D), 1.0),
        "ctx": nrm(ks[2], (BATCH, CTX_LEN, D), 1.0),
        "c_ctx": nrm(ks[3], (D,), 1.0),
        "ada_w": nrm(ks[4], (DEPTH, D, 6 * D), 0.5 * D ** -0.5),
        "ada_b": nrm(ks[5], (DEPTH, 6 * D), 0.02),
        "norm_mix_w": 1.0 + nrm(ks[6], (DEPTH, D), 0.02),
        "norm_ffn_w": 1.0 + nrm(ks[7], (DEPTH, D), 0.02),
        "ev_w_in": nrm(ks[8], (N_EVEN, D, EV_IN), D ** -0.5),
        "ev_w_out": nrm(ks[9], (N_EVEN, EV_MIX, D), EV_MIX ** -0.5),
        "na_rpb": nrm(ks[10], (N_EVEN, NA_HEADS, 2 * NA_KH - 1, 2 * NA_KW - 1), 0.1),
        "hg_lb_logits": nrm(ks[11], (N_EVEN + 1, 2, HG_KEY), 0.1),
        "hg_norm_w": 1.0 + nrm(ks[12], (N_EVEN, HG_VAL), 0.02),
        "od_w_in": nrm(ks[13], (N_ODD, D, 3 * D), D ** -0.5),
        "od_conv_w": nrm(ks[14], (N_ODD, CONV_W, D), CONV_W ** -0.5),
        "od_conv_b": nrm(ks[15], (N_ODD, D), 0.02),
        "od_w_out": nrm(ks[16], (N_ODD, D, D), D ** -0.5),
        "ffn_w_up": nrm(ks[17], (DEPTH, D, 2 * D_FF_2), D ** -0.5),
        "ffn_conv_w": nrm(ks[18], (DEPTH, CONV_W, D_FF_2), CONV_W ** -0.5),
        "ffn_conv_b": nrm(ks[19], (DEPTH, D_FF_2), 0.02),
        "ffn_w_down": nrm(ks[20], (DEPTH, D_FF_2, D), D_FF_2 ** -0.5),
        "final_norm_w": 1.0 + nrm(ks[21], (D,), 0.02),
    }

def second_block(x, c, ctx, c_ctx, ada_w, ada_b, norm_mix_w, norm_ffn_w, ev_w_in, ev_w_out,
              na_rpb, hg_lb_logits, hg_norm_w, od_w_in, od_conv_w, od_conv_b, od_w_out,
              ffn_w_up, ffn_conv_w, ffn_conv_b, ffn_w_down, final_norm_w):
    lb_all = jnp.cumsum(jax.nn.softmax(hg_lb_logits.astype(jnp.float32), axis=0), axis=0)[:N_EVEN]
    silu_c = jax.nn.silu(c)
    silu_cc = jax.nn.silu(c_ctx)[None]
    xc = ctx
    for layer in range(DEPTH):
        j = layer // 2
        is_even = layer % 2 == 0
        ctx_feeds_later = any(l % 2 == 0 for l in range(layer + 1, DEPTH))
        mod = silu_c @ ada_w[layer] + ada_b[layer]
        shift_m, scale_m, gate_m, shift_f, scale_f, gate_f = jnp.split(mod, 6, axis=-1)
        if is_even or ctx_feeds_later:
            mod_c = silu_cc @ ada_w[layer] + ada_b[layer]
            cshift_m, cscale_m, cgate_m, cshift_f, cscale_f, cgate_f = jnp.split(mod_c, 6, axis=-1)
            h_ctx = modulate(rms_norm(xc, norm_mix_w[layer]), cshift_m, cscale_m)
        h = modulate(rms_norm(x, norm_mix_w[layer]), shift_m, scale_m)
        if is_even:
            y, y_ctx = even_mixer(h, h_ctx, ev_w_in[j], ev_w_out[j], na_rpb[j], lb_all[j],
                                  hg_norm_w[j], ctx_feeds_later)
        else:
            y = short_conv_mixer(h, od_w_in[j], od_conv_w[j], od_conv_b[j], od_w_out[j])
            y_ctx = (short_conv_mixer(h_ctx, od_w_in[j], od_conv_w[j], od_conv_b[j], od_w_out[j])
                     if ctx_feeds_later else None)
        x = x + gate_m[:, None, :] * y
        h = modulate(rms_norm(x, norm_ffn_w[layer]), shift_f, scale_f)
        x = x + gate_f[:, None, :] * conv_ffn_2(h, ffn_w_up[layer], ffn_conv_w[layer],
                                              ffn_conv_b[layer], ffn_w_down[layer])
        if ctx_feeds_later:
            xc = xc + cgate_m[:, None, :] * y_ctx
            hc = modulate(rms_norm(xc, norm_ffn_w[layer]), cshift_f, cscale_f)
            xc = xc + cgate_f[:, None, :] * conv_ffn_2(hc, ffn_w_up[layer], ffn_conv_w[layer],
                                                     ffn_conv_b[layer], ffn_w_down[layer])
    return rms_norm(x, final_norm_w)


def setup_inputs(seed=0):
    out = dict(first_inputs(seed))
    for name, value in second_inputs(seed + 1).items():
        if name != "x":
            out[name + "_2"] = value
    return out


def reference(
    x, mem, norm_mix_g, norm_ffn_g, a_w_in, a_gate_b, a_conv_w, a_conv_b, a_head_g, a_w_out,
    kv_norm_g, w_kv, b_w_in, b_rel_bias, b_w_out, mem_w_kv, ffn_w_up, ffn_conv_w, ffn_conv_b,
    ffn_w_down, final_g, c_2, ctx_2, c_ctx_2, ada_w_2, ada_b_2, norm_mix_w_2, norm_ffn_w_2,
    ev_w_in_2, ev_w_out_2, na_rpb_2, hg_lb_logits_2, hg_norm_w_2, od_w_in_2, od_conv_w_2,
    od_conv_b_2, od_w_out_2, ffn_w_up_2, ffn_conv_w_2, ffn_conv_b_2, ffn_w_down_2,
    final_norm_w_2,
):
    x = first_block(
        x, mem, norm_mix_g, norm_ffn_g, a_w_in, a_gate_b, a_conv_w, a_conv_b, a_head_g, a_w_out,
        kv_norm_g, w_kv, b_w_in, b_rel_bias, b_w_out, mem_w_kv, ffn_w_up, ffn_conv_w,
        ffn_conv_b, ffn_w_down, final_g,
    )
    return second_block(
        x, c_2, ctx_2, c_ctx_2, ada_w_2, ada_b_2, norm_mix_w_2, norm_ffn_w_2, ev_w_in_2,
        ev_w_out_2, na_rpb_2, hg_lb_logits_2, hg_norm_w_2, od_w_in_2, od_conv_w_2, od_conv_b_2,
        od_w_out_2, ffn_w_up_2, ffn_conv_w_2, ffn_conv_b_2, ffn_w_down_2, final_norm_w_2,
    )


_drawn_inputs = setup_inputs


def setup_inputs(seed=0):
    import zlib

    import numpy as np

    out = dict(_drawn_inputs(seed))
    spreads = {}
    factors = {'a_conv_b': 6.293,
     'ffn_conv_b': 3.687,
     'norm_mix_w_2': 4.556,
     'norm_ffn_w_2': 5.873,
     'na_rpb_2': 8.0,
     'hg_lb_logits_2': 8.0,
     'hg_norm_w_2': 8.0,
     'od_conv_b_2': 64.0,
     'ffn_conv_b_2': 8.0,
     'final_norm_w_2': 8.228}
    for name, (base, spread) in spreads.items():
        noise = np.random.default_rng([zlib.crc32(name.encode()), seed]).standard_normal(out[name].shape)
        drawn = base * np.exp(spread * noise) if base else spread * noise
        out[name] = __import__('jax').numpy.asarray(drawn.astype(out[name].dtype))
    for name, factor in factors.items():
        out[name] = (out[name] * factor).astype(out[name].dtype)
    return out
```

```python
import concourse.bass as bass
from concourse import mybir
from contextlib import ExitStack

FP = mybir.dt.float32
FR = mybir.dt.float32r
U32 = mybir.dt.uint32
ACT = mybir.ActivationFunctionType
ALU = mybir.AluOpType
AXX = mybir.AxisListType.X

P = 128
D = 1024
KB = D // P
T = 256
EPS = 1e-6
FF = 2816
NI = FF // 256
RING = 3
NEG = -1e30
MH, MD = 4, 192
BH = 12
HGH = 4
CH = 32
NCH = T // CH

STREAM = [
    ("mk0", 1, "fm", "ctx"), ("mv0", 1, "tm", "ctx"), ("mk1", 1, "fm", "ctx"), ("mv1", 1, "tm", "ctx"),
    ("a_qk", 6, "fm", "lat"), ("a_v", 3, "tm", "lat"), ("a_o", 3, "fm", "lat"), ("a_qm", 1, "fm", "lat"),
    ("a_out", 4, "fm", "mix"), ("ffn0", 3 * NI, "ffn", "lat"),
    ("kv_k", 3, "fm", "lat"), ("kv_v", 3, "tm", "lat"), ("b_q", 3, "fm", "lat"), ("b_qm", 1, "fm", "lat"),
    ("b_out", 4, "fm", "mix"), ("ffn1", 3 * NI, "ffn", "lat"),
    ("e_ff", 2, "fm2", "both"), ("e_fb", 2, "fm2", "both"), ("e_hi", 2, "tm2", "both"),
    ("e_hq", 2, "fm", "lat"), ("e_hg", 2, "fm", "lat"),
    ("e_nq", 2, "fm", "lat"), ("e_nk", 2, "fm2", "both"), ("e_nv", 2, "tm2", "both"),
    ("e_out", 4, "fm", "mix"), ("ffn2", 3 * NI, "ffn", "lat"),
    ("o_b", 4, "fm", "lat"), ("o_cu", 8, "fm", "lat"), ("o_out", 4, "fm", "mix"), ("ffn3", 3 * NI, "ffn", "lat"),
]


class Job:
    def __init__(self, unit, kind, half, src, number, banked):
        self.unit, self.kind, self.half, self.src = unit, kind, half, src
        self.number, self.banked = number, banked


def plan():
    jobs, unit, number, banked, last = {}, 0, 0, 0, []
    for name, units, kind, src in STREAM:
        out = []
        for u in range(units):
            for half in range(2 if kind.endswith("2") else 1):
                fills = not (kind == "ffn" and ffn_kind(u) == "down")
                out.append(Job(unit + u, kind, half, src, number, banked if fills else None))
                number += 1
                banked += fills
            last.append(number)
        jobs[name] = out
        unit += units
    return jobs, unit, last


def ffn_kind(u):
    if u < 2:
        return ("g", "u")[u]
    return ("g", "u", "down")[(u - 2) % 3] if u < 3 * NI - 1 else "down"


JOBS, NU, LAST = plan()

VECS = {}
_at = 0
for _n, _w in [("mix_g", 16), ("ffn_g", 16), ("kv_g", 8), ("fin_g", 8), ("mix_w2", 16), ("ffn_w2", 16),
               ("fin_w2", 8), ("a_conv", 60), ("a_head", 6), ("ffn_conv", 4 * NI * 8), ("od_conv", 32),
               ("ada_b", 96), ("hg_lb", 16), ("hg_w", 4), ("cc", 16), ("gate_b", 8)]:
    VECS[_n] = (_at, _w)
    _at += _w
NVEC = _at
CONS = {}
_at = 0
for _n, _w in [("ident", 128), ("flip", 128), ("causal", 128), ("row4", 4), ("na", 64)]:
    CONS[_n] = (_at, _w)
    _at += _w
NCON = _at
HCONS = {"m_f": (0, T), "m_b": (T, T), "scan_f": (512, 512), "scan_b": (1024, 512)}



def build(nc, io, out):
    JN = JOBS
    with ExitStack() as ctx:
        def sb(name, shape, dt=FP):
            return ctx.enter_context(nc.sbuf_tensor(name, shape, dt))

        def sem(name):
            return ctx.enter_context(nc.semaphore(name))

        raw = [sb(f"raw{i}", [P, 2048]) for i in range(RING)]
        whi = [sb(f"whi{i}", [P, 2048], FR) for i in range(RING)]
        wlo = [sb(f"wlo{i}", [P, 2048], FR) for i in range(RING)]
        ada = sb("ada", [P, KB, 256])
        x = sb("x", [P, KB, T])
        t = sb("t", [P, KB, T])
        h_hi = sb("h_hi", [P, KB, 512], FR)
        h_lo = sb("h_lo", [P, KB, 512], FR)
        mix_hi = sb("mix_hi", [P, KB, T], FR)
        mix_lo = sb("mix_lo", [P, KB, T], FR)
        hd_hi = sb("hd_hi", [P, 2, T], FR)
        hd_lo = sb("hd_lo", [P, 2, T], FR)
        vec = sb("vec", [P, NVEC])
        con = sb("con", [P, NCON])
        ones = sb("ones", [P, T])
        gw = sb("gw", [P, KB, 8])
        lb = sb("lb", [P, 4, 2, HGH])
        rs = sb("rs", [P, T])
        var = sb("var", [P, T])
        sc = sb("sc", [P, KB, 2])
        mod = sb("mod", [P, 2, 48, 2])
        gain = sb("gain", [P, 5, KB])
        arena_floats = 12928
        arena = sb("arena", [P, arena_floats])

        def area(at, *shape):
            n = 1
            for s in shape:
                n *= s
            assert at + n <= arena_floats, (at, n)
            a = arena[:, at:at + n]
            if len(shape) == 1:
                return a
            if len(shape) == 2:
                return a.rearrange("p (a b) -> p a b", b=shape[1])
            return a.rearrange("p (a b c) -> p a b c", b=shape[1], c=shape[2])

        def idle(at, *shape):
            a = t[:].rearrange("p k n -> p (k n)")[:, at:at + (shape[0] * shape[1] if len(shape) > 1 else shape[0])]
            return a.rearrange("p (a b) -> p a b", b=shape[1]) if len(shape) > 1 else a

        g_row = idle(0, 6, T)
        b_p = [idle(512, 256), idle(768, 256)]
        b_t = [idle(1024, 256), idle(1280, 256)]
        s_am = [idle(1536, T), idle(1792, T)]
        small = [sb(f"small{i}", [P, 4]) for i in range(2)]
        s_dec = sb("s_dec", [P, NCH])

        mkv = area(0, 2, 2, 512)
        sq = area(arena_floats - KB * T, KB, T)
        aq = area(2048, 6, T)
        ak = area(3584, 6, T)
        av = area(5120, 2, 768)
        ao = area(6656, 6, T)
        qm = area(8192, 2, T)
        m_arg = area(8704, 384)
        m_e = area(9088, 384)
        m_p = area(9472, 384)
        m_em = area(9856, T)
        m_d = area(10112, T)
        m_d2 = area(10368, T)
        m_sq = area(10624, 2, T)
        m_hm = area(11136, 2, T)
        m_y = [m_sq, m_hm]
        g_tm = area(11648, 2, 8)
        g_col = area(11664, 2, 4)
        m_sel = area(11672, 4, P)
        f_y = area(8704, 2, T)
        f_s = area(9216, 2, T)
        f_h = area(9728, 2, T)
        bk = area(2048, 6, T)
        bv = area(3584, 2, 768)
        bq = area(5120, 6, T)
        bqm = area(6656, 2, T)
        band = area(7168, BH, 384)
        ctxx = area(0, KB, T)
        hf = [area(0, HGH, 512), area(2048, HGH, 512)]
        hv = area(4096, 4, 512)
        hq = area(6144, HGH, T)
        hg = area(7168, HGH, T)
        s_fg = area(8192, 512)
        s_b = area(8704, 512)
        s_bs = area(8704, 512)
        s_bd = area(9216, 512)
        s_q = area(9728, T)
        s_k = area(9984, T)
        s_kt = area(10240, 4, P)
        s_st = area(10752, NCH, P)
        s_vb = area(11776, 2, 512)
        nbias = area(0, 48, 64)
        nq = area(3072, 4, T)
        nk = area(4096, 4, 512)
        nv = area(6144, 4, 512)
        n_p = [area(9216, 512), area(9728, 512)]
        n_t = [area(10240, 512), area(10752, 512)]
        ogb = area(0, KB, T)
        ogc = area(2048, 2, T)
        ocu = area(2560, 2, T)
        ocv = area(3072, 2, T)

        def vc(name, c=0, n=1):
            at = VECS[name][0] + c
            return vec[:, at:at + n]

        def cn(name):
            if name in HCONS:
                return idle(*HCONS[name])
            at, w = CONS[name]
            return con[:, at:at + w]

        def psum(name):
            return ctx.enter_context(nc.psum_tensor(name, [P, 512], FP))

        L = [psum("L0"), psum("L1")]
        Dn = [psum(f"D{i}") for i in range(4)]
        M0 = psum("M0")
        N0 = psum("N0")
        ident = cn("ident")

        def tile(h, qb, q, k, w, v, mix, bufs, bias=None, nb=0):
            pr = (h % 2) * 64
            return dict(w=w, pr=pr, qb=qb, mix=mix + h // 2, bias=bias, nb=nb, v=v, p=bufs[0],
                        t=bufs[1], q=q[pr:pr + 64, h // 2, qb * P:qb * P + P], k=k(slice(pr, pr + 64), h // 2, w))

        def memory_tiles(layer, q):
            return [tile(h, qb, q, lambda p, c, w: mkv[p, layer, 0, c * T:c * T + w], T,
                         [mkv[:, layer, 1, kb * 256 + h * 64:kb * 256 + h * 64 + 64] for kb in range(2)],
                         6, (b_p, b_t)) for h in range(4) for qb in range(2)]

        T_A = memory_tiles(0, qm)
        T_B = [tile(h, qb, bq, lambda p, c, w: bk[p, c, 0:w], P * (qb + 1),
                    [bv[:, kb, h * 64:h * 64 + 64] for kb in range(qb + 1)], 0, (b_p, b_t),
                    band[:, h, P * qb:P * qb + P * (qb + 1)], P * (qb + 1))
               for h in range(BH) for qb in range(2)] + memory_tiles(1, bqm)
        T_N = [tile(h, qb, nq, lambda p, c, w: nk[p, c, 0:w], 512,
                    [nv[:, kb, h * 64:h * 64 + 64] for kb in range(4)], 0, (n_p, n_t),
                    nbias[:, h * 6 + 2 - 2 * qb:h * 6 + 6 - 2 * qb, :].rearrange("p a b -> p (a b)"), T)
               for h in range(8) for qb in range(2)]
        OB = [N0, L[0]]

        ld = {n: sem(f"ld_{n}") for n in ("x", "mem", "vec", "con", "gate", "ctx", "band", "nbias", "hcons")}
        raw_full = [sem(f"raw_full{i}") for i in range(RING)]
        ada_full, ada_used = sem("ada_full"), sem("ada_used")
        unit_hi, unit_lo = sem("unit_hi"), sem("unit_lo")
        job_done, job_evac = sem("job_done"), sem("job_evac")
        out_done = sem("out_done")
        dve_step, act_step = sem("dve_step"), sem("act_step")
        R = {n: sem(n) for n in (
            "ones_set", "cc_ready", "ctx_hi", "ctx_lo", "sq_done", "ss_done", "rv_done", "rs_done", "t_done",
            "h_hi_done", "h_lo_done", "x_ready", "mod_ready", "q_silu", "o_sig",
            "gate_tm", "gate_sum", "gate_T", "gate_in", "gate_e", "gate_l", "row_ready", "em_exp", "em_ready",
            "acol_T", "acol_ready", "ml_s", "ml_arg", "ml_e", "ml_mask", "ml_p", "ml_num", "ml_sq", "ml_ss",
            "ml_rv", "ml_rs", "ml_h", "mix_hi_done", "mix_lo_done", "ffn_act", "hdh_done", "hdl_done", "down_done",
            "at_sc", "at_max", "at_exp", "at_nrm", "at_tp", "at_pt", "at_o", "bias_ready", "hgf_sig", "hgq_silu",
            "lb_in", "lb_exp", "hg_fg", "hg_g", "hg_b", "hg_bd", "hg_e", "hg_kd", "hg_att", "hg_kdt",
            "hg_am", "hg_u", "hg_st", "hg_o", "hg_sq", "hg_ss", "hg_rv", "hg_rs", "hg_h", "od_h")}

        MIX = {"ml": 2 * MH, "memA": 2 * MH + 2, "B": 2 * MH + 10, "hg": 2 * MH + 14, "na": 2 * MH + 18,
               "od": 2 * MH + 22}
        N_FINAL = 11

        def pieces(h):
            b = 3 * (h // 2)
            return (b, b + 1, 0) if h % 2 == 0 else (b + 2, b + 1, 64)

        def evacuated(name):
            j = JOBS[name][0]
            return j.banked

        def finished(name):
            return JOBS[name][-1].number + 1

        block = ctx.enter_context(nc.Block())

        @block.sync
        def _(sp):
            for v in range(RING):
                sp.dma_start(raw[v][:], io["units"][v]).then_inc(raw_full[v], 16)
            whole = NU // RING
            with sp.Fori(1, whole) as g:
                for r in range(RING):
                    sp.wait_ge(unit_lo, RING * g + (r + 1 - RING))
                    sp.dma_start(raw[r][:], io["units"][bass.ds(RING * g + r, 1)].rearrange("a p n -> (a p) n")) \
                        .then_inc(raw_full[r], 16)
            for v in range(whole * RING, NU):
                sp.wait_ge(unit_lo, v - RING + 1)
                sp.dma_start(raw[v % RING][:], io["units"][v]).then_inc(raw_full[v % RING], 16)
            for k in range(KB):
                sp.wait_ge(R["t_done"], KB * N_FINAL + k + 1)
                sp.dma_start(out[:, k, :], t[:, k, :]).then_inc(out_done, 16)
            sp.wait_ge(out_done, 16 * KB)

        @block.gpsimd
        def _(gp):
            def ada_load(n):
                gp.wait_ge(ada_used, n)
                gp.dma_start(ada[:].rearrange("p k n -> p (k n)"),
                             io["ada"][bass.ds(n, 1)].rearrange("a p n -> (a p) n")).then_inc(ada_full, 16)

            def windows(ap, pattern):
                return bass.AP(tensor=ap.tensor, offset=ap.offset, ap=pattern)

            nc.gpsimd.memset(ones[:], 1.0).then_inc(R["ones_set"], 1)
            gp.dma_start(ada[:].rearrange("p k n -> p (k n)"), io["ada"][0]).then_inc(ada_full, 16)
            gp.wait_ge(ld["con"], 16)
            for h in range(MH):
                gp.wait_ge(R["ml_e"], h + 1)
                for c in (0, T):
                    nc.gpsimd.tensor_tensor(m_e[:, c:c + P], m_e[:, c:c + P], cn("causal"), ALU.mult) \
                        .then_inc(R["ml_mask"], 1)
            with gp.Fori(1, NI) as n:
                ada_load(n)
            gp.wait_ge(R["rs_done"], 3)
            for h in range(BH):
                for qb in range(2):
                    w = P * (qb + 1)
                    gp.dma_start(band[:, h, P * qb:P * qb + w],
                                 windows(io["relx"][h, P * (1 - qb):256], [[1, P], [1, w]])) \
                        .then_inc(ld["band"], 16)
            with gp.Fori(NI, 2 * NI + 2) as n:
                ada_load(n)
            gp.wait_ge(R["hdl_done"], 2 * NI)
            gp.dma_start(ctxx, io["ctx"]).then_inc(ld["ctx"], 16)
            gp.wait_ge(R["h_lo_done"], KB * 7)
            gp.dma_start(t[:].rearrange("p k n -> p (k n)")[:, 0:1536], io["hcons"]).then_inc(ld["hcons"], 16)
            with gp.Fori(2 * NI + 2, 37) as n:
                ada_load(n)
            gp.wait_ge(R["mix_lo_done"], MIX["hg"])
            for half in range(2):
                for h in range(8):
                    gp.dma_start(nbias[64 - 64 * half:128 - 64 * half, 6 * h:6 * h + 6, :],
                                 windows(io["nax"][h, 1 - half, 0:64], [[1, 64], [127, 6], [1, 64]])) \
                        .then_inc(ld["nbias"], 16)
            with gp.Fori(37, 48) as n:
                ada_load(n)

        @block.scalar
        def _(act):
            A = nc.scalar
            made, stats, applied, rounded = [0], [0], [0], [0]

            def hi(v):
                s = v % RING
                act.wait_ge(raw_full[s], 16 * (v // RING + 1))
                if v >= RING:
                    act.wait_ge(job_done, LAST[v - RING])
                A.activation(whi[s][:], raw[s][:], ACT.Copy).then_inc(unit_hi, 1)

            def upto(v):
                while made[0] <= min(v, NU - 1):
                    hi(made[0])
                    made[0] += 1

            def jobs(name, after=None):
                for n, j in enumerate(JOBS[name]):
                    upto(j.unit + 2)
                    if after:
                        act.wait_ge(job_evac, j.banked + 1)
                        after(n, j)

            def stat(src, ready):
                for i in range(4):
                    act.wait_ge(*ready(i))
                    A.activation(sq[:, 2 * i:2 * i + 2, :], src[:, 2 * i:2 * i + 2, :], ACT.Square) \
                        .then_inc(R["sq_done"], 1)
                stats[0] += 1
                act.wait_ge(R["rv_done"], stats[0])
                A.activation(rs[:], var[:], ACT.Sqrt).then_inc(R["rs_done"], 1)

            def apply(shift=None, col=0, before=None):
                base = KB * applied[0]
                applied[0] += 1
                if before:
                    act.wait_ge(job_done, before)
                for k in range(KB):
                    act.wait_ge(R["t_done"], base + k + 1)
                    dst = h_hi[:, k, col:col + T]
                    if shift is None:
                        A.activation(dst, t[:, k, :], ACT.Copy).then_inc(R["h_hi_done"], 1)
                    else:
                        A.activation(dst, t[:, k, :], ACT.Identity, bias=shift(k)).then_inc(R["h_hi_done"], 1)

            def evac_parts(name):
                return lambda i: (job_evac, JOBS[name][0].banked + i + 1)

            def ffn_parts(n):
                return lambda i: (R["x_ready"], 4 * n + i + 1)

            def attention(tl, t0, g0):
                n = len(tl)
                for i in range(n + 4):
                    if i < n:
                        a, g = tl[i], t0 + i
                        act.wait_ge(R["at_max"], g + 1)
                        if g >= 2:
                            act.wait_ge(R["at_tp"], g - 1)
                        A.activation(a["p"][g % 2][:, 0:a["w"]], Dn[g % 2][:, 0:a["w"]], ACT.Exp, bias=small[g % 2][:, 0:1],
                                     accum_out=small[g % 2][:, 1:2]).then_inc(R["at_exp"], 1)
                    if 0 <= i - 1 < n:
                        a, g = tl[i - 1], t0 + i - 1
                        act.wait_ge(R["at_tp"], g + 1)
                        if g >= 2:
                            act.wait_ge(R["at_o"], g - 1)
                        A.activation(a["t"][g % 2][:, 0:a["w"]], Dn[2 + g % 2][:, 0:a["w"]], ACT.Copy) \
                            .then_inc(R["at_pt"], 1)
                    if 3 <= i < n + 3 and (i - 3) % 4 == 3:
                        gg = (i - 3) // 4
                        act.wait_ge(R["at_o"], t0 + i - 2)
                        A.activation(mix_hi[:, tl[i - 3]["mix"], :], OB[(g0 + gg) % 2][:, 0:T], ACT.Copy) \
                            .then_inc(R["mix_hi_done"], 1)

            def ffn(name, f, func):
                j0, u0, b0 = JOBS[name][0].number, JOBS[name][0].unit, JOBS[name][0].banked

                def wh(r, i):
                    s = (u0 + r) % RING
                    act.wait_ge(raw_full[s], i * 16 + 16 * ((u0 + r) // RING + 1))
                    act.wait_ge(job_done, i * 3 + (j0 + r - RING + 1))
                    A.activation(whi[s][:], raw[s][:], ACT.Copy).then_inc(unit_hi, 1)

                def gate(i):
                    act.wait_ge(job_evac, i * 2 + (b0 + 1))
                    A.activation(f_s, f_y, func).then_inc(R["ffn_act"], 1)

                def hidden(i, down):
                    act.wait_ge(job_evac, i * 2 + (b0 + 2))
                    if down is not None:
                        act.wait_ge(job_done, down)
                    A.activation(hd_hi[:], f_h, ACT.Copy).then_inc(R["hdh_done"], 1)

                upto(u0 + 2)
                gate(0)
                upto(u0 + 3)
                hidden(0, None)
                upto(u0 + 4)
                gate(1)
                upto(u0 + 5)
                upto(u0 + 6)
                hidden(1, j0 + 5)
                with act.Fori(2, NI - 1) as i:
                    wh(1, i)
                    gate(i)
                    wh(2, i)
                    wh(3, i)
                    hidden(i, i * 3 + (j0 + 2))
                made[0] = u0 + 3 * (NI - 1) + 1
                i = NI - 1
                upto(u0 + 3 * i + 1)
                gate(i)
                upto(u0 + 3 * i + 2)
                upto(u0 + 3 * i + 3)
                hidden(i, i * 3 + (j0 + 2))

            act.dma_start(t[:], io["mem"]).then_inc(ld["mem"], 16)
            act.dma_start(x[:], io["x"]).then_inc(ld["x"], 16)
            act.dma_start(vec[:], io["vecs"]).then_inc(ld["vec"], 16)
            act.dma_start(gw[:], io["gate"]).then_inc(ld["gate"], 16)
            act.dma_start(con[:], io["cons"]).then_inc(ld["con"], 16)

            act.wait_ge(ld["mem"], 16)
            A.activation(h_hi[:, :, T:512], t[:], ACT.Copy).then_inc(R["ctx_hi"], 1)
            upto(1)
            act.wait_ge(ld["vec"], 16)
            A.activation(sc[:].rearrange("p k n -> p (k n)"), vc("cc", 0, 16), ACT.Silu).then_inc(R["cc_ready"], 1)
            stat(x, lambda i: (ld["x"], 16))
            for name in ("mk0", "mv0", "mk1", "mv1"):
                jobs(name)
            apply()

            def q_silu(n, j):
                dst = (aq if n < 3 else ak)[:, 2 * (n % 3):2 * (n % 3) + 2, :]
                A.activation(dst, m_y[n % 2], ACT.Silu).then_inc(R["q_silu"], 1)

            def o_sig(n, j):
                dst = ao[:, 2 * n:2 * n + 2, :]
                A.activation(dst, dst, ACT.Sigmoid).then_inc(R["o_sig"], 1)

            jobs("a_qk", q_silu)
            jobs("a_v")
            jobs("a_o", o_sig)
            jobs("a_qm")
            act.wait_ge(R["gate_in"], 1)
            A.activation(g_row[0:4, 2, :], g_row[0:4, 2, :], ACT.Exp).then_inc(R["gate_e"], 1)
            act.wait_ge(R["gate_e"], 1)
            A.activation(g_row[0:4, 2, :], g_row[0:4, 2, :], ACT.Ln, bias=1.0).then_inc(R["gate_l"], 1)
            act.wait_ge(R["row_ready"], 1)
            A.activation(g_row[0:4, 5, :], g_row[0:4, 5, :], ACT.Exp, scale=-1.0).then_inc(R["em_exp"], 1)
            for h in range(MH):
                full, half, pr = pieces(h)
                act.wait_ge(R["ml_arg"], h + 1)
                if h:
                    act.wait_ge(R["ml_p"], h)
                A.activation(m_e, m_arg, ACT.Exp).then_inc(R["ml_e"], 1)
                act.wait_ge(R["ml_num"], h + 1)
                A.activation(m_sq[:, 0, :], Dn[2][:, 0:T], ACT.Square).then_inc(R["ml_sq"], 1)
                A.activation(m_sq[pr:pr + 64, 1, :], Dn[2][pr:pr + 64, T:512], ACT.Square).then_inc(R["ml_sq"], 1)
                act.wait_ge(R["ml_rv"], h + 1)
                A.activation(rs[:], var[:], ACT.Sqrt).then_inc(R["ml_rs"], 1)
                act.wait_ge(R["ml_h"], 2 * h + 2)
                A.activation(mix_hi[:, full, :], m_hm[:, 0, :], ACT.Copy).then_inc(R["mix_hi_done"], 1)
                A.activation(mix_hi[pr:pr + 64, half, :], m_hm[pr:pr + 64, 1, :], ACT.Copy) \
                    .then_inc(R["mix_hi_done"], 1)
            attention(T_A, 0, 0)
            jobs("a_out")
            stat(x, evac_parts("a_out"))
            apply()
            ffn("ffn0", 0, ACT.Silu)

            stat(x, ffn_parts(0))
            apply(before=finished("ffn0"))
            jobs("kv_k")
            jobs("kv_v")
            apply(before=finished("kv_v"))
            jobs("b_q")
            jobs("b_qm")
            attention(T_B, len(T_A), 2)
            jobs("b_out")
            stat(x, evac_parts("b_out"))
            apply()
            ffn("ffn1", 1, ACT.Silu)

            stat(x, ffn_parts(1))
            applied[0] += 1
            stat(ctxx, lambda i: (ld["ctx"], 16))
            act.wait_ge(R["mod_ready"], 1)
            apply(lambda k: mod[:, 0, k, 1:2], T)
            stat(x, lambda i: (R["t_done"], KB * 5 + 2 * i + 2))
            apply(lambda k: mod[:, 0, k, 0:1])

            def f_sig(d):
                def run(n, j):
                    A.activation(hf[d][:, n, :], hf[d][:, n, :], ACT.Sigmoid).then_inc(R["hgf_sig"], 1)
                return run

            def hq_silu(dst):
                def run(n, j):
                    A.activation(dst[:, 2 * n:2 * n + 2, :], dst[:, 2 * n:2 * n + 2, :], ACT.Silu) \
                        .then_inc(R["hgq_silu"], 1)
                return run

            jobs("e_ff", f_sig(0))
            jobs("e_fb", f_sig(1))
            jobs("e_hi")
            jobs("e_hq", hq_silu(hq))
            jobs("e_hg", hq_silu(hg))
            act.wait_ge(R["lb_in"], 1)
            A.activation(lb[:, 0:2], lb[:, 0:2], ACT.Exp).then_inc(R["lb_exp"], 1)
            for e in range(2 * HGH):
                h, d = e // 2, e % 2
                act.wait_ge(R["hg_fg"], e + 1)
                A.activation(s_b, s_fg, ACT.Ln).then_inc(R["hg_g"], 1)
                act.wait_ge(R["hg_b"], e + 1)
                if e:
                    act.wait_ge(R["hg_o"], e)
                A.activation(s_q, s_bs[:, 0:T], ACT.Exp).then_inc(R["hg_e"], 1)
                A.activation(s_k, s_bs[:, 0:T], ACT.Exp, scale=-1.0).then_inc(R["hg_e"], 1)
                ends = s_bs[:, CH - 1:T:CH] if d == 0 else s_bs[:, 0:T:CH]
                A.activation(s_dec[:], ends, ACT.Exp).then_inc(R["hg_e"], 1)
                act.wait_ge(R["hg_bd"], e + 1)
                A.activation(s_bd, s_bd, ACT.Exp).then_inc(R["hg_e"], 1)
                act.wait_ge(R["hg_att"], e + 1)
                A.activation(s_kt.rearrange("p a b -> p (a b)"), Dn[1][:], ACT.Copy).then_inc(R["hg_kdt"], 1)
                if d == 1:
                    act.wait_ge(R["hg_o"], e + 1)
                    A.activation(s_bd[:, 0:T], L[0][:, 0:T], ACT.Square).then_inc(R["hg_sq"], 1)
                    act.wait_ge(R["hg_rv"], h + 1)
                    A.activation(rs[:], var[:], ACT.Sqrt).then_inc(R["hg_rs"], 1)
                    act.wait_ge(R["hg_h"], h + 1)
                    A.activation(mix_hi[:, 4 + h, :], s_bd[:, 0:T], ACT.Copy).then_inc(R["mix_hi_done"], 1)
            jobs("e_nq")
            jobs("e_nk")
            jobs("e_nv")
            attention(T_N, len(T_A) + len(T_B), 10)
            jobs("e_out")
            stat(x, evac_parts("e_out"))
            apply(lambda k: mod[:, 0, 24 + k, 0:1])
            ffn("ffn2", 2, ACT.Gelu)

            stat(x, ffn_parts(2))
            act.wait_ge(R["mod_ready"], 2)
            apply(lambda k: mod[:, 1, k, 0:1])
            jobs("o_b")

            def o_round(n, j):
                if n % 2:
                    act.wait_ge(R["od_h"], n // 2 + 1)
                    A.activation(mix_hi[:, n - 1:n + 1, :], ocv, ACT.Copy).then_inc(R["mix_hi_done"], 1)

            jobs("o_cu", o_round)
            jobs("o_out")
            stat(x, evac_parts("o_out"))
            apply(lambda k: mod[:, 1, 24 + k, 0:1])
            ffn("ffn3", 3, ACT.Gelu)
            stat(x, ffn_parts(3))

        @block.vector
        def _(dve):
            V = nc.vector
            steps, made, stats, applied, rounded = [0], [0], [0], [0], [0]

            def step(ins):
                ins.then_inc(dve_step, 1)
                steps[0] = steps[0] + 1

            def sync():
                dve.wait_ge(dve_step, steps[0])

            def lo(v):
                s = v % RING
                dve.wait_ge(unit_hi, v + 1)
                V.tensor_tensor(wlo[s][:], raw[s][:], whi[s][:].bitcast(FP), ALU.subtract).then_inc(unit_lo, 1)

            def upto(v):
                while made[0] <= min(v, NU - 1):
                    lo(made[0])
                    made[0] += 1

            def bank(j):
                return L[j.banked % 2]

            def jobs(name, evac):
                for n, j in enumerate(JOBS[name]):
                    upto(j.unit + 2)
                    dve.wait_ge(job_done, j.number + 1)
                    evac(n, j, bank(j)).then_inc(job_evac, 1)

            def pair(ap):
                return ap.rearrange("p (a b) -> p a b", b=T)

            def stat(dim=D):
                dve.wait_ge(R["ss_done"], stats[0] + 1)
                stats[0] += 1
                step(V.tensor_scalar(var[:], N0[:, 0:T], 1.0 / dim, EPS, ALU.mult, ALU.add))
                sync()
                V.reciprocal(var[:], var[:]).then_inc(R["rv_done"], 1)

            def apply(g, src=None, dst=None, shift=None, col=0, before=None, to_h=True):
                src = x if src is None else src
                dst = t if dst is None else dst
                dve.wait_ge(R["rs_done"], stats[0])
                if before:
                    dve.wait_ge(job_done, before)
                for k in range(KB + 1):
                    if k < KB:
                        V.scalar_tensor_tensor(dst[:, k, :], src[:, k, :], g(k), rs[:], ALU.mult, ALU.mult) \
                            .then_inc(R["t_done"], 1)
                    if to_h and k:
                        q = k - 1
                        dve.wait_ge(R["h_hi_done"], rounded[0] + q + 1)
                        a, b = h_lo[:, q, col:col + T], h_hi[:, q, col:col + T].bitcast(FP)
                        if shift is None:
                            V.tensor_tensor(a, t[:, q, :], b, ALU.subtract).then_inc(R["h_lo_done"], 1)
                        else:
                            V.scalar_tensor_tensor(a, t[:, q, :], shift(q), b, ALU.add, ALU.subtract) \
                                .then_inc(R["h_lo_done"], 1)
                applied[0] += 1
                if to_h:
                    rounded[0] += KB

            def conv(y, src, taps, bias, offsets):
                for n, (w, o) in enumerate(zip(taps, offsets)):
                    for c in range(2):
                        if n == 0:
                            ins = V.tensor_scalar(y[:, c, :], src[:, c, :], w(c), bias(c), ALU.mult, ALU.add)
                        else:
                            a, b = (0, T - o) if o > 0 else (-o, T)
                            d = y[:, c, o:T] if o > 0 else y[:, c, 0:T + o]
                            ins = V.scalar_tensor_tensor(d, src[:, c, a:b], w(c), d, ALU.mult, ALU.add)
                        if n == len(taps) - 1 and c == 1:
                            return ins
                        step(ins)
                    sync()

            def attention(tl, t0, g0, mixbase):
                n = len(tl)
                for i in range(n + 4):
                    if i < n:
                        a, g = tl[i], t0 + i
                        dve.wait_ge(R["at_sc"], g + 1)
                        V.tensor_reduce(small[g % 2][:, 0:1], Dn[g % 2][:, 0:a["w"]], AXX, ALU.max, negate=True) \
                            .then_inc(R["at_max"], 1)
                    if 0 <= i - 1 < n:
                        a, g = tl[i - 1], t0 + i - 1
                        dve.wait_ge(R["at_exp"], g + 1)
                        step(V.reciprocal(small[g % 2][:, 2:3], small[g % 2][:, 1:2]))
                        sync()
                        p = a["p"][g % 2][:, 0:a["w"]]
                        V.tensor_scalar(p, p, small[g % 2][:, 2:3], None, ALU.mult).then_inc(R["at_nrm"], 1)
                    if 3 <= i < n + 3 and (i - 3) % 4 == 3:
                        gg = (i - 3) // 4
                        m = tl[i - 3]["mix"]
                        dve.wait_ge(R["mix_hi_done"], mixbase + gg + 1)
                        V.tensor_tensor(mix_lo[:, m, :], OB[(g0 + gg) % 2][:, 0:T], mix_hi[:, m, :].bitcast(FP),
                                        ALU.subtract).then_inc(R["mix_lo_done"], 1)

            def residual(name, gate=None):
                def evac(n, j, b):
                    if gate is None:
                        dst = x[:, 2 * n:2 * n + 2, :]
                        return V.tensor_tensor(dst, dst, pair(b[:]), ALU.add)
                    d = [x[:, 2 * n + c, :] for c in range(2)]
                    step(V.scalar_tensor_tensor(d[0], b[:, 0:T], gate(2 * n), d[0], ALU.mult, ALU.add))
                    return V.scalar_tensor_tensor(d[1], b[:, T:512], gate(2 * n + 1), d[1], ALU.mult, ALU.add)
                jobs(name, evac)

            def ffn(name, f, offsets, gate=None):
                j0, u0, b0 = JOBS[name][0].number, JOBS[name][0].unit, JOBS[name][0].banked
                at = VECS["ffn_conv"][0] + 8 * NI * f
                g_bank, u_bank = L[b0 % 2], L[(b0 + 1) % 2]

                def wl(r, i):
                    s = (u0 + r) % RING
                    dve.wait_ge(unit_hi, i * 3 + (u0 + r + 1))
                    V.tensor_tensor(wlo[s][:], raw[s][:], whi[s][:].bitcast(FP), ALU.subtract).then_inc(unit_lo, 1)

                def tap(i, n):
                    def col(c):
                        o = i * 8 + (at + 4 * c + n)
                        return vec[:, o:o + 1] if isinstance(i, int) else vec[:, bass.ds(o, 1)]
                    return col

                def convolve(i, g_job):
                    dve.wait_ge(job_done, g_job + 1)
                    conv(f_y, pair(g_bank[:]), [tap(i, n) for n in range(3)], tap(i, 3), offsets) \
                        .then_inc(job_evac, 1)

                def multiply(i, u_job):
                    dve.wait_ge(job_done, u_job + 1)
                    dve.wait_ge(R["ffn_act"], i + (f * NI + 1))
                    V.tensor_tensor(f_h, f_s, pair(u_bank[:]), ALU.mult).then_inc(job_evac, 1)

                def hidden(i):
                    dve.wait_ge(R["hdh_done"], i + (f * NI + 1))
                    V.tensor_tensor(hd_lo[:], f_h, hd_hi[:].bitcast(FP), ALU.subtract).then_inc(R["hdl_done"], 1)

                upto(u0 + 2)
                convolve(0, j0)
                upto(u0 + 3)
                multiply(0, j0 + 1)
                hidden(0)
                upto(u0 + 4)
                convolve(1, j0 + 2)
                upto(u0 + 5)
                multiply(1, j0 + 3)
                upto(u0 + 6)
                hidden(1)
                n0 = steps[0]
                per = 5
                with dve.Fori(2, NI - 1) as i:
                    steps[0] = (i - 2) * per + n0
                    wl(1, i)
                    convolve(i, i * 3 + (j0 - 1))
                    wl(2, i)
                    multiply(i, i * 3 + j0)
                    wl(3, i)
                    hidden(i)
                steps[0] = n0 + per * (NI - 3)
                made[0] = u0 + 3 * (NI - 1) + 1
                i = NI - 1
                upto(u0 + 3 * i + 1)
                convolve(i, j0 + 3 * i - 1)
                upto(u0 + 3 * i + 2)
                multiply(i, j0 + 3 * i)
                upto(u0 + 3 * i + 3)
                hidden(i)
                dve.wait_ge(job_done, finished(name))
                for n in range(4):
                    if gate is None:
                        dst = x[:, 2 * n:2 * n + 2, :]
                        V.tensor_tensor(dst, dst, pair(Dn[n][:]), ALU.add).then_inc(R["x_ready"], 1)
                    else:
                        for c in range(2):
                            dst = x[:, 2 * n + c, :]
                            ins = V.scalar_tensor_tensor(dst, Dn[n][:, c * T:c * T + T], gate(2 * n + c), dst,
                                                         ALU.mult, ALU.add)
                            if c:
                                ins.then_inc(R["x_ready"], 1)
                            else:
                                step(ins)

            CAUSAL3, CENTRED3 = (0, 1, 2), (0, 1, -1)

            dve.wait_ge(R["ctx_hi"], 1)
            V.tensor_tensor(h_lo[:, :, T:512], t[:], h_hi[:, :, T:512].bitcast(FP), ALU.subtract) \
                .then_inc(R["ctx_lo"], 1)
            upto(1)
            stat()

            def to_mkv(layer, which):
                return lambda n, j, b: V.tensor_copy(mkv[:, layer, which, :], b[:])

            for layer in range(2):
                jobs(f"mk{layer}", to_mkv(layer, 0))
                jobs(f"mv{layer}", to_mkv(layer, 1))
            apply(lambda k: vc("mix_g", k))

            def qk_conv(n, j, b):
                if n >= 2:
                    dve.wait_ge(R["q_silu"], n - 1)
                at = VECS["a_conv"][0] + 10 * n
                return conv(m_y[n % 2], pair(b[:]),
                            [(lambda c, o=o: vec[:, at + 5 * c + o:at + 5 * c + o + 1]) for o in range(4)],
                            lambda c: vec[:, at + 5 * c + 4:at + 5 * c + 5], (0, 1, 2, 3))

            jobs("a_qk", qk_conv)
            jobs("a_v", lambda n, j, b: V.tensor_copy(av[:, :, 256 * n:256 * n + 256], pair(b[:])))
            jobs("a_o", lambda n, j, b: V.tensor_copy(ao[:, 2 * n:2 * n + 2, :], pair(b[:])))
            jobs("a_qm", lambda n, j, b: V.tensor_scalar(qm, pair(b[:]), 0.125, None, ALU.mult))
            dve.wait_ge(R["gate_tm"], 1)
            V.tensor_tensor(g_tm, N0[:, 0:16].rearrange("p (a b) -> p a b", b=8),
                            vc("gate_b", 0, 8).unsqueeze(1).to_broadcast([P, 2, 8]), ALU.add) \
                .then_inc(R["gate_sum"], 1)
            dve.wait_ge(R["gate_T"], 1)
            g4 = [g_row[0:4, i, :] for i in range(6)]
            step(V.tensor_copy(g_row[0:4, 0:2, :], N0[0:4, :].rearrange("p (a b) -> p a b", b=T)))
            sync()
            V.scalar_tensor_tensor(g4[2], g4[1], -1.0, g4[1], ALU.mult, ALU.min).then_inc(R["gate_in"], 1)
            step(V.tensor_scalar(g4[1], g4[1], 0.0, None, ALU.min))
            sync()
            dve.wait_ge(R["gate_l"], 1)
            step(V.tensor_tensor(g4[1], g4[1], g4[2], ALU.subtract))
            sync()
            step(V.tensor_tensor_scan(g4[3], ones[0:4, :], g4[1], 0.0, ALU.mult, ALU.add))
            sync()
            step(V.tensor_tensor(g4[0], g4[0], g4[3], ALU.subtract))
            sync()
            step(V.tensor_tensor_scan(g4[4], g4[0], g4[0], 0.0, ALU.max, ALU.max))
            sync()
            step(V.tensor_tensor(g4[5], g4[3], g4[4], ALU.add))
            sync()
            V.tensor_scalar(g4[4], g4[4], -1.0, None, ALU.mult).then_inc(R["row_ready"], 1)
            dve.wait_ge(R["acol_T"], 1)
            for h in range(MH):
                step(V.tensor_copy(m_sel[0:4, h, :], ident[0:4, h:h + 1].to_broadcast([4, P])))
            step(V.tensor_copy(g_col.rearrange("p a b -> p (a b)"), N0[:, 0:8]))
            dve.wait_ge(R["em_exp"], 1)
            V.tensor_scalar(g4[5], g4[5], 1e18, None, ALU.min).then_inc(R["em_ready"], 1)
            sync()
            for h in range(MH):
                full, half, pr = pieces(h)
                dve.wait_ge(R["ml_s"], h + 1)
                step(V.tensor_copy(m_em, Dn[1][:, T:512]))
                step(V.tensor_scalar(m_arg[:, 0:T], Dn[1][:, 0:T], g_col[:, 0, h:h + 1], 0.0, ALU.add, ALU.min))
                V.tensor_scalar(m_arg[:, T:T + P], Dn[1][:, P:T], g_col[:, 1, h:h + 1], 0.0, ALU.add, ALU.min) \
                    .then_inc(R["ml_arg"], 1)
                dve.wait_ge(R["ml_mask"], 2 * h + 2)
                V.scalar_tensor_tensor(m_p, Dn[0][:, 0:384], MD ** -0.5, m_e, ALU.mult, ALU.mult) \
                    .then_inc(R["ml_p"], 1)
                dve.wait_ge(R["ml_num"], h + 1)
                sync()
                step(V.scalar_tensor_tensor(m_d, Dn[3][:, 0:T], -1.0, m_em, ALU.mult, ALU.max))
                sync()
                step(V.scalar_tensor_tensor(m_d, Dn[3][:, 0:T], 1.0, m_d, ALU.mult, ALU.max))
                sync()
                step(V.scalar_tensor_tensor(m_d2, m_d, EPS, m_d, ALU.mult, ALU.mult))
                sync()
                dve.wait_ge(R["ml_ss"], h + 1)
                step(V.scalar_tensor_tensor(var[:], N0[:, 0:T], 1.0 / MD, m_d2, ALU.mult, ALU.add))
                sync()
                step(V.tensor_scalar(var[:], var[:], 1e-34, 1e34, ALU.max, ALU.min))
                sync()
                V.reciprocal(var[:], var[:]).then_inc(R["ml_rv"], 1)
                dve.wait_ge(R["ml_rs"], h + 1)
                dve.wait_ge(R["o_sig"], 3)
                step(V.scalar_tensor_tensor(m_hm[:, 0, :], Dn[2][:, 0:T], vc("a_head", full), rs[:],
                                            ALU.mult, ALU.mult))
                hp = slice(pr, pr + 64)
                step(V.scalar_tensor_tensor(m_hm[hp, 1, :], Dn[2][hp, T:512], vc("a_head", half)[hp], rs[hp, :],
                                            ALU.mult, ALU.mult))
                sync()
                V.tensor_tensor(m_hm[:, 0, :], m_hm[:, 0, :], ao[:, full, :], ALU.mult).then_inc(R["ml_h"], 1)
                V.tensor_tensor(m_hm[hp, 1, :], m_hm[hp, 1, :], ao[hp, half, :], ALU.mult).then_inc(R["ml_h"], 1)
                dve.wait_ge(R["mix_hi_done"], 2 * h + 2)
                V.tensor_tensor(mix_lo[:, full, :], m_hm[:, 0, :], mix_hi[:, full, :].bitcast(FP), ALU.subtract) \
                    .then_inc(R["mix_lo_done"], 1)
                V.tensor_tensor(mix_lo[hp, half, :], m_hm[hp, 1, :], mix_hi[hp, half, :].bitcast(FP),
                                ALU.subtract).then_inc(R["mix_lo_done"], 1)
                dve.wait_ge(R["mix_lo_done"], 2 * h + 2)
            attention(T_A, 0, 0, MIX["ml"])
            residual("a_out")
            stat()
            apply(lambda k: vc("ffn_g", k))
            ffn("ffn0", 0, CAUSAL3)

            stat()
            apply(lambda k: vc("kv_g", k), before=finished("ffn0"))
            jobs("kv_k", lambda n, j, b: V.tensor_copy(bk[:, 2 * n:2 * n + 2, :], pair(b[:])))
            jobs("kv_v", lambda n, j, b: V.tensor_copy(bv[:, :, 256 * n:256 * n + 256], pair(b[:])))
            apply(lambda k: vc("mix_g", KB + k), before=finished("kv_v"))
            jobs("b_q", lambda n, j, b: V.tensor_scalar(bq[:, 2 * n:2 * n + 2, :], pair(b[:]), 0.125, None, ALU.mult))
            jobs("b_qm", lambda n, j, b: V.tensor_scalar(bqm, pair(b[:]), 0.125, None, ALU.mult))
            dve.wait_ge(ld["band"], 16 * 2 * BH)
            V.memset(band[64:128, :, 64:128], NEG).then_inc(R["bias_ready"], 1)
            V.memset(band[64:128, :, P + 192:P + 256], NEG).then_inc(R["bias_ready"], 1)
            attention(T_B, len(T_A), 2, MIX["memA"])
            residual("b_out")
            stat()
            apply(lambda k: vc("ffn_g", KB + k))
            ffn("ffn1", 1, CAUSAL3)

            def modulation(layer, gains):
                dve.wait_ge(ada_used, 24 * (layer + 1))
                bias = vc("ada_b", 48 * layer, 48).unsqueeze(2).to_broadcast([P, 48, 2])
                step(V.tensor_tensor(mod[:, layer, :, :],
                                     M0[:, 96 * layer:96 * layer + 96].rearrange("p (a b) -> p a b", b=2),
                                     bias, ALU.add))
                sync()
                for n, (slot, blk, c, name, at) in enumerate(gains):
                    ins = V.scalar_tensor_tensor(gain[:, slot, :], mod[:, layer, blk:blk + KB, c], 1.0,
                                                 vc(name, at, KB), ALU.add, ALU.mult)
                    if n == len(gains) - 1:
                        ins.then_inc(R["mod_ready"], 1)
                    else:
                        step(ins)
                dve.wait_ge(R["mod_ready"], layer + 1)

            stat()
            apply(lambda k: vc("fin_g", k), dst=x, to_h=False)
            modulation(0, [(0, 8, 1, "mix_w2", 0), (1, 8, 0, "mix_w2", 0), (2, 32, 0, "ffn_w2", 0)])
            stat()
            apply(lambda k: gain[:, 0, k:k + 1], src=ctxx, shift=lambda k: mod[:, 0, k, 1:2], col=T)
            stat()
            dve.wait_ge(R["h_lo_done"], rounded[0])
            apply(lambda k: gain[:, 1, k:k + 1], shift=lambda k: mod[:, 0, k, 0:1])
            for d, name in ((0, "e_ff"), (1, "e_fb")):
                jobs(name, lambda n, j, b, d=d: V.tensor_copy(hf[d][:, n, :], b[:]))
            jobs("e_hi", lambda n, j, b: V.tensor_copy(hv[:, 2 * (n % 2):2 * (n % 2) + 2, 256 * (n // 2):256 * (n // 2) + 256],
                                                       pair(b[:])))
            jobs("e_hq", lambda n, j, b: V.tensor_copy(hq[:, 2 * n:2 * n + 2, :], pair(b[:])))
            jobs("e_hg", lambda n, j, b: V.tensor_copy(hg[:, 2 * n:2 * n + 2, :], pair(b[:])))
            lg = vc("hg_lb", 0, 16).rearrange("p (l d h) -> p l d h", l=2, d=2)
            step(V.tensor_tensor(lb[:, 2], lg[:, 0], lg[:, 1], ALU.max))
            sync()
            step(V.tensor_tensor(lb[:, 0], lg[:, 0], lb[:, 2], ALU.subtract))
            V.tensor_tensor(lb[:, 1], lg[:, 1], lb[:, 2], ALU.subtract).then_inc(R["lb_in"], 1)
            dve.wait_ge(R["lb_exp"], 1)
            step(V.tensor_tensor(lb[:, 3], lb[:, 0], lb[:, 1], ALU.add))
            sync()
            step(V.reciprocal(lb[:, 3], lb[:, 3]))
            sync()
            step(V.tensor_tensor(lb[:, 2], lb[:, 0], lb[:, 3], ALU.mult))
            sync()
            step(V.tensor_scalar(lb[:, 3], lb[:, 2], -1.0, 1.0, ALU.mult, ALU.add))
            step(V.memset(s_am[0], 0.0))
            step(V.memset(s_am[1], 0.0))
            sync()
            dve.wait_ge(ld["hcons"], 16)
            dve.wait_ge(R["hgf_sig"], 2 * HGH)
            dve.wait_ge(R["hgq_silu"], 4)
            for e in range(2 * HGH):
                h, d = e // 2, e % 2
                if d == 0:
                    for tb in range(2):
                        for c in range(4):
                            step(V.tensor_scalar(s_vb[:, tb, c * P:c * P + P], hv[:, tb, h * P:h * P + P],
                                                 cn("row4")[:, c:c + 1], None, ALU.mult))
                V.tensor_scalar(s_fg, hf[d][:, h, :], lb[:, 3, d, h:h + 1], lb[:, 2, d, h:h + 1],
                                ALU.mult, ALU.add).then_inc(R["hg_fg"], 1)
                dve.wait_ge(R["hg_g"], e + 1)
                fwd = d == 0
                order = (lambda ap: ap) if fwd else (lambda ap: ap[:, ::-1])
                V.tensor_tensor_scan(order(s_bs), order(cn("scan_f" if fwd else "scan_b")), order(s_b), 0.0,
                                     ALU.mult, ALU.add).then_inc(R["hg_b"], 1)
                step(V.tensor_scalar(s_fg, s_fg, -1.0, 1.0, ALU.mult, ALU.add))
                dve.wait_ge(R["hg_b"], e + 1)
                c3 = s_bs[:, 0:T].rearrange("p (c n) -> p c n", n=CH)
                end = c3[:, :, CH - 1:CH] if fwd else c3[:, :, 0:1]
                cend = s_bs[:, 511:512] if fwd else s_bs[:, T:T + 1]
                step(V.tensor_tensor(s_bd[:, 0:T].rearrange("p (c n) -> p c n", n=CH),
                                     end.to_broadcast([P, NCH, CH]), c3, ALU.subtract))
                V.tensor_tensor(s_bd[:, T:512], cend.to_broadcast([P, T]), s_bs[:, T:512], ALU.subtract) \
                    .then_inc(R["hg_bd"], 1)
                sync()
                dve.wait_ge(R["hg_e"], 4 * e + 4)
                step(V.tensor_tensor(s_q, s_q, hq[:, h, :], ALU.mult))
                step(V.tensor_tensor(s_k, s_k, s_fg[:, 0:T], ALU.mult))
                V.tensor_tensor(s_bd, s_bd, s_fg, ALU.mult).then_inc(R["hg_kd"], 1)
                dve.wait_ge(R["hg_att"], e + 1)
                V.copy_predicated(s_am[d], cn("m_f" if fwd else "m_b").bitcast(U32), Dn[0][:, 0:T]) \
                    .then_inc(R["hg_am"], 1)
                chunks = list(range(NCH)) if fwd else list(range(NCH))[::-1]
                dve.wait_ge(R["hg_u"], e + 1)
                step(V.tensor_copy(s_st[:, chunks[0], :], N0[:, 0:P]))
                sync()
                for a, b in zip(chunks[:-1], chunks[1:]):
                    ins = V.scalar_tensor_tensor(s_st[:, b, :], s_st[:, a, :], s_dec[:, a:a + 1],
                                                 Dn[2 + a // 4][:, (a % 4) * P:(a % 4) * P + P], ALU.mult, ALU.add)
                    if b == chunks[-1]:
                        ins.then_inc(R["hg_st"], 1)
                        dve.wait_ge(R["hg_st"], e + 1)
                    else:
                        step(ins)
                        sync()
                if d == 1:
                    dve.wait_ge(R["hg_ss"], h + 1)
                    step(V.tensor_scalar(var[:], L[1][:, 0:T], 1.0 / P, EPS, ALU.mult, ALU.add))
                    sync()
                    V.reciprocal(var[:], var[:]).then_inc(R["hg_rv"], 1)
                    dve.wait_ge(R["hg_rs"], h + 1)
                    step(V.scalar_tensor_tensor(s_bd[:, T:512], L[0][:, 0:T], vc("hg_w", h), rs[:],
                                                ALU.mult, ALU.mult))
                    sync()
                    V.tensor_tensor(s_bd[:, 0:T], s_bd[:, T:512], hg[:, h, :], ALU.mult).then_inc(R["hg_h"], 1)
                    dve.wait_ge(R["mix_hi_done"], MIX["B"] + h + 1)
                    V.tensor_tensor(mix_lo[:, 4 + h, :], s_bd[:, 0:T], mix_hi[:, 4 + h, :].bitcast(FP),
                                    ALU.subtract).then_inc(R["mix_lo_done"], 1)
            dve.wait_ge(R["mix_lo_done"], MIX["hg"])
            jobs("e_nq", lambda n, j, b: V.tensor_scalar(nq[:, 2 * n:2 * n + 2, :], pair(b[:]), 0.125, None, ALU.mult))
            jobs("e_nk", lambda n, j, b: V.tensor_copy(nk[:, n, :], b[:]))
            jobs("e_nv", lambda n, j, b: V.tensor_copy(nv[:, 2 * (n % 2):2 * (n % 2) + 2, 256 * (n // 2):256 * (n // 2) + 256],
                                                       pair(b[:])))
            dve.wait_ge(ld["nbias"], 16 * 16)
            V.tensor_tensor(nbias, nbias, cn("na").unsqueeze(1).to_broadcast([P, 48, 64]), ALU.add) \
                .then_inc(R["bias_ready"], 1)
            attention(T_N, len(T_A) + len(T_B), 10, MIX["hg"])
            residual("e_out", lambda k: mod[:, 0, 16 + k, 0:1])
            stat()
            apply(lambda k: gain[:, 2, k:k + 1], shift=lambda k: mod[:, 0, 24 + k, 0:1])
            ffn("ffn2", 2, CENTRED3, lambda k: mod[:, 0, 40 + k, 0:1])

            modulation(1, [(3, 8, 0, "mix_w2", KB), (4, 32, 0, "ffn_w2", KB)])
            stat()
            apply(lambda k: gain[:, 3, k:k + 1], shift=lambda k: mod[:, 1, k, 0:1])
            jobs("o_b", lambda n, j, b: V.tensor_copy(ogb[:, 2 * n:2 * n + 2, :], pair(b[:])))

            def c_or_u(n, j, b):
                if n % 2 == 0:
                    return V.tensor_copy(ogc, pair(b[:]))
                return V.tensor_tensor(ocu, ogc, pair(b[:]), ALU.mult)

            def short_conv(n):
                dve.wait_ge(job_evac, JOBS["o_cu"][2 * n + 1].banked + 1)
                at = VECS["od_conv"][0] + 8 * n
                if n:
                    dve.wait_ge(R["mix_lo_done"], MIX["na"] + n)
                step(conv(ocv, ocu, [(lambda c, o=o: vec[:, at + 4 * c + o:at + 4 * c + o + 1]) for o in range(3)],
                          lambda c: vec[:, at + 4 * c + 3:at + 4 * c + 4], CENTRED3))
                sync()
                V.tensor_tensor(ocv, ocv, ogb[:, 2 * n:2 * n + 2, :], ALU.mult).then_inc(R["od_h"], 1)
                dve.wait_ge(R["mix_hi_done"], MIX["na"] + n + 1)
                V.tensor_tensor(mix_lo[:, 2 * n:2 * n + 2, :], ocv, mix_hi[:, 2 * n:2 * n + 2, :].bitcast(FP),
                                ALU.subtract).then_inc(R["mix_lo_done"], 1)

            for n, j in enumerate(JOBS["o_cu"]):
                upto(j.unit + 2)
                dve.wait_ge(job_done, j.number + 1)
                c_or_u(n, j, bank(j)).then_inc(job_evac, 1)
                dve.wait_ge(job_evac, j.banked + 1)
                if n % 2:
                    short_conv(n // 2)
            residual("o_out", lambda k: mod[:, 1, 16 + k, 0:1])
            stat()
            apply(lambda k: gain[:, 4, k:k + 1], shift=lambda k: mod[:, 1, 24 + k, 0:1])
            ffn("ffn3", 3, CENTRED3, lambda k: mod[:, 1, 40 + k, 0:1])
            stat()
            apply(lambda k: vc("fin_w2", k), to_h=False)

        @block.tensor
        def _(pe):
            mm = nc.tensor.matmul
            stats, h_in, ada_n = [0], [0], [0]

            def mm3(dst, w, h, start, stop):
                for n, (a, b) in enumerate(((0, 0), (0, 1), (1, 0))):
                    ins = mm(dst, w[a], h[b], start=start and n == 0, stop=stop and n == 2, skip_group_check=True)
                return ins

            def job(j, first=False, h_base=None):
                s = j.unit % RING
                w = [r[s][:].rearrange("p (k n) -> p k n", n=256) for r in (whi, wlo)]
                rows = (mix_hi, mix_lo) if j.src == "mix" else (h_hi, h_lo)
                c0, cw = {"lat": (0, T), "mix": (0, T), "ctx": (T, T), "both": (0, 512)}[j.src]
                pe.wait_ge(unit_lo, j.unit + 1)
                if j.banked >= 2:
                    pe.wait_ge(job_evac, j.banked - 1)
                b = L[j.banked % 2]
                for part in range(1 if j.kind == "fm2" else 2):
                    for k in range(KB):
                        if first and part == 0 and h_base is not None:
                            pe.wait_ge(R["h_lo_done"], h_base + k + 1)
                        if j.kind in ("fm", "ffn"):
                            dst = b[:, part * T:part * T + T]
                            W = [q[:, k, part * P:part * P + P] for q in w]
                            H = [q[:, k, c0:c0 + cw] for q in rows]
                        elif j.kind == "fm2":
                            dst = b[:]
                            W = [q[:, k, j.half * P:j.half * P + P] for q in w]
                            H = [q[:, k, :] for q in rows]
                        else:
                            dst = b[:, part * 256:part * 256 + 256]
                            at = (c0 if j.kind == "tm" else j.half * T) + part * P
                            W = [q[:, k, at:at + P] for q in rows]
                            H = [q[:, k, :] for q in w]
                        ins = mm3(dst, W, H, k == 0, k == KB - 1)
                ins.then_inc(job_done, 1)

            def jobs(name, fresh=False, ada=0):
                for n, j in enumerate(JOBS[name]):
                    job(j, n == 0, h_in[0] if fresh else None)
                    if n == 0 and fresh:
                        h_in[0] += KB
                    if n < ada:
                        modulate(ada_n[0])
                        ada_n[0] += 1

            def modulate(n):
                pe.wait_ge(ada_full, 16 * (n + 1))
                for c in range(2):
                    at = n * 4 + 2 * c
                    dst = M0[:, at:at + 2] if isinstance(n, int) else M0[:, bass.ds(at, 2)]
                    for k in range(KB):
                        ins = mm(dst, ada[:, k, c * P:c * P + P], sc[:, k, :], start=k == 0, stop=k == KB - 1,
                                 skip_group_check=True)
                ins.then_inc(ada_used, 1)

            def stat():
                for k in range(KB):
                    if k % 2 == 0:
                        pe.wait_ge(R["sq_done"], 4 * stats[0] + k // 2 + 1)
                    ins = mm(N0[:, 0:T], ones[:, 0:P], sq[:, k, :], start=k == 0, stop=k == KB - 1)
                ins.then_inc(R["ss_done"], 1)
                stats[0] += 1

            def attention(tl, t0, g0, mixbase):
                n = len(tl)
                for i in range(n + 2):
                    if i < n:
                        a, g = tl[i], t0 + i
                        if g >= 2:
                            pe.wait_ge(R["at_exp"], g - 1)
                        ins = mm(Dn[g % 2][:, 0:a["w"]], a["q"], a["k"], start=True, stop=a["bias"] is None)
                        if a["bias"] is not None:
                            ins = mm(Dn[g % 2][:, 0:a["nb"]], cn("flip"), a["bias"], start=False, stop=True)
                        ins.then_inc(R["at_sc"], 1)
                    if 0 <= i - 1 < n:
                        a, g = tl[i - 1], t0 + i - 1
                        pe.wait_ge(R["at_nrm"], g + 1)
                        if g >= 2:
                            pe.wait_ge(R["at_pt"], g - 1)
                        for kb in range(a["w"] // P):
                            ins = nc.tensor.transpose(Dn[2 + g % 2][:, kb * P:kb * P + P],
                                                      a["p"][g % 2][:, kb * P:kb * P + P], ident)
                        ins.then_inc(R["at_tp"], 1)
                    if i >= 2:
                        a, g = tl[i - 2], t0 + i - 2
                        gg = (i - 2) // 4
                        pe.wait_ge(R["at_pt"], g + 1)
                        if (i - 2) % 4 == 0 and gg >= 2:
                            pe.wait_ge(R["mix_lo_done"], mixbase + gg - 1)
                        pr, c = a["pr"], a["qb"] * P
                        dst = OB[(g0 + gg) % 2][pr:pr + 64, c:c + P]
                        for kb, v in enumerate(a["v"]):
                            ins = mm(dst, v, a["t"][g % 2][:, kb * P:kb * P + P], start=kb == 0,
                                     stop=kb == len(a["v"]) - 1)
                        ins.then_inc(R["at_o"], 1)

            def ffn(name, f, ada=True):
                jl = JOBS[name]
                j0, u0, b0 = jl[0].number, jl[0].unit, jl[0].banked

                def chunk(r, i, which):
                    s = (u0 + r) % RING
                    pe.wait_ge(unit_lo, i * 3 + (u0 + r + 1))
                    pe.wait_ge(job_evac, i * 2 + (b0 + which - 1))
                    b = L[(b0 + which) % 2]
                    w = [q[s][:].rearrange("p (k n) -> p k n", n=256) for q in (whi, wlo)]
                    for part in range(2):
                        for k in range(KB):
                            ins = mm3(b[:, part * T:part * T + T], [q[:, k, part * P:part * P + P] for q in w],
                                      [q[:, k, 0:T] for q in (h_hi, h_lo)], k == 0, k == KB - 1)
                    ins.then_inc(job_done, 1)

                def down(r, i, first=False, last=False):
                    s = (u0 + r) % RING
                    if last:
                        pe.wait_ge(unit_lo, u0 + 3 * NI)
                    else:
                        pe.wait_ge(unit_lo, i * 3 + (u0 + r + 1))
                    pe.wait_ge(R["hdl_done"], i + (f * NI + (1 if last else 0)))
                    w = [q[s][:].rearrange("p (k n) -> p k n", n=D) for q in (whi, wlo)]
                    for kt in range(2):
                        for c in range(KB):
                            dst = Dn[c // 2][:, (c % 2) * T:(c % 2) * T + T]
                            ins = mm3(dst, [q[:, kt, c * P:c * P + P] for q in w],
                                      [q[:, kt, :] for q in (hd_hi, hd_lo)],
                                      first and kt == 0 and c % 2 == 0, last and kt == 1)
                    ins.then_inc(job_done, 1)

                def mod_step(n):
                    if ada:
                        modulate(n)

                n0 = ada_n[0]
                job(jl[0], True, h_in[0])
                h_in[0] += KB
                mod_step(n0)
                job(jl[1])
                job(jl[2])
                mod_step(n0 + 1)
                job(jl[3])
                down(1, 1, first=True)
                with pe.Fori(2, NI - 1) as i:
                    chunk(-1, i, 0)
                    chunk(0, i, 1)
                    mod_step(i + n0)
                    down(1, i)
                i = NI - 1
                chunk(-1, i, 0)
                chunk(0, i, 1)
                mod_step(n0 + i)
                down(1, i)
                down(3 * NI - 1, i, last=True)
                if ada:
                    ada_n[0] += NI

            pe.wait_ge(R["ones_set"], 1)
            stat()
            pe.wait_ge(R["ctx_lo"], 1)
            for name in ("mk0", "mv0", "mk1", "mv1"):
                jobs(name)

            jobs("a_qk", fresh=True)
            jobs("a_v")
            jobs("a_o")
            jobs("a_qm")
            pe.wait_ge(ld["gate"], 16)
            for tb in range(2):
                for k in range(KB):
                    ins = mm(N0[:, 8 * tb:8 * tb + 8], t[:, k, tb * P:tb * P + P], gw[:, k, :],
                             start=k == 0, stop=k == KB - 1)
            ins.then_inc(R["gate_tm"], 1)
            pe.wait_ge(ld["con"], 16)
            pe.wait_ge(R["gate_sum"], 1)
            for which in range(2):
                for tb in range(2):
                    ins = nc.tensor.transpose(N0[0:4, which * T + tb * P:which * T + tb * P + P],
                                              g_tm[:, tb, 4 * which:4 * which + 4], ident)
            ins.then_inc(R["gate_T"], 1)
            pe.wait_ge(R["row_ready"], 1)
            for tb in range(2):
                ins = nc.tensor.transpose(N0[:, 4 * tb:4 * tb + 4], g_row[0:4, 0, tb * P:tb * P + P],
                                          ident[0:4, 0:4])
            ins.then_inc(R["acol_T"], 1)
            pe.wait_ge(R["em_ready"], 1)
            pe.wait_ge(R["q_silu"], 6)
            for h in range(MH):
                full, half, pr = pieces(h)
                hp = slice(pr, pr + 64)
                sel = m_sel[0:4, h, :]
                if h:
                    pe.wait_ge(R["ml_p"], h)
                mm(Dn[1][:, 0:T], sel, g_row[0:4, 4, :], start=True, stop=True)
                mm(Dn[1][:, T:512], sel, g_row[0:4, 5, :], start=True, stop=True)
                for sb_, (c, w) in enumerate(((0, T), (T, P))):
                    q0 = T - w
                    mm(Dn[0][:, c:c + w], ak[:, full, sb_ * P:sb_ * P + P], aq[:, full, q0:T],
                       start=True, stop=False)
                    ins = mm(Dn[0][:, c:c + w], ak[hp, half, sb_ * P:sb_ * P + P], aq[hp, half, q0:T],
                             start=False, stop=True)
                ins.then_inc(R["ml_s"], 1)
                pe.wait_ge(R["ml_p"], h + 1)
                if h:
                    pe.wait_ge(R["ml_h"], 2 * h)

                def weighted(dst, lhs):
                    mm(dst, lhs(0), m_p[:, 0:T], start=True, stop=False)
                    return mm(dst[:, P:T], lhs(1), m_p[:, T:T + P], start=False, stop=True)

                weighted(Dn[2][:, 0:T], lambda s: av[:, s, full * P:full * P + P])
                weighted(Dn[2][hp, T:512], lambda s: av[:, s, half * P + pr:half * P + pr + 64])
                weighted(Dn[3][:, 0:T], lambda s: ones[:, 0:P]).then_inc(R["ml_num"], 1)
                pe.wait_ge(R["ml_sq"], 2 * h + 2)
                mm(N0[:, 0:T], ones[:, 0:P], m_sq[:, 0, :], start=True, stop=False)
                mm(N0[:, 0:T], ones[hp, 0:P], m_sq[hp, 1, :], start=False, stop=True).then_inc(R["ml_ss"], 1)
            pe.wait_ge(R["mix_lo_done"], MIX["ml"])
            pe.wait_ge(job_evac, evacuated("a_out"))
            attention(T_A, 0, 0, MIX["ml"])
            pe.wait_ge(R["mix_lo_done"], MIX["memA"])
            jobs("a_out")
            stat()
            pe.wait_ge(R["cc_ready"], 1)
            ffn("ffn0", 0)

            stat()
            jobs("kv_k", fresh=True, ada=2)
            jobs("kv_v")
            jobs("b_q", fresh=True)
            jobs("b_qm")
            pe.wait_ge(job_evac, evacuated("b_out"))
            pe.wait_ge(R["bias_ready"], 2)
            attention(T_B, len(T_A), 2, MIX["memA"])
            pe.wait_ge(R["mix_lo_done"], MIX["B"])
            jobs("b_out")
            stat()
            ffn("ffn1", 1)

            stat()
            stat()
            stat()
            h_in[0] += KB
            pe.wait_ge(R["mod_ready"], 1)
            jobs("e_ff", fresh=True, ada=4)
            jobs("e_fb", ada=4)
            jobs("e_hi", ada=4)
            jobs("e_hq", ada=1)
            jobs("e_hg")
            for e in range(2 * HGH):
                h, d = e // 2, e % 2
                pe.wait_ge(R["hg_kd"], e + 1)
                for tb in range(2):
                    mm(Dn[0][:, tb * P:tb * P + P], s_k[:, tb * P:tb * P + P], s_q[:, tb * P:tb * P + P],
                       start=True, stop=True)
                for b in range(4):
                    ins = nc.tensor.transpose(Dn[1][:, b * P:b * P + P], s_bd[:, b * P:b * P + P], ident)
                ins.then_inc(R["hg_att"], 1)
                pe.wait_ge(R["hg_kdt"], e + 1)
                for tb in range(2):
                    mm(N0[:, 0:P], s_kt[:, 2 + tb, :], hv[:, 2 + tb, h * P:h * P + P], start=tb == 0, stop=tb == 1)
                for tb in range(2):
                    ins = mm(Dn[2 + tb][:], s_kt[:, tb, :], s_vb[:, tb, :], start=True, stop=True)
                ins.then_inc(R["hg_u"], 1)
                pe.wait_ge(R["hg_am"], e + 1)
                pe.wait_ge(R["hg_st"], e + 1)
                if d == 0 and h:
                    pe.wait_ge(R["mix_lo_done"], MIX["B"] + h)
                for tb in range(2):
                    mm(L[0][:, tb * P:tb * P + P], hv[:, tb, h * P:h * P + P], s_am[d][:, tb * P:tb * P + P],
                       start=d == 0 and tb == 0, stop=False, skip_group_check=True)
                for c in range(NCH):
                    ins = mm(L[0][:, c * CH:c * CH + CH], s_st[:, c, :], s_q[:, c * CH:c * CH + CH],
                             start=False, stop=d == 1 and c == NCH - 1, skip_group_check=True)
                ins.then_inc(R["hg_o"], 1)
                if d == 1:
                    pe.wait_ge(R["hg_sq"], h + 1)
                    mm(L[1][:, 0:T], ones[:, 0:P], s_bd[:, 0:T], start=True, stop=True).then_inc(R["hg_ss"], 1)
            pe.wait_ge(R["mix_lo_done"], MIX["hg"])
            jobs("e_nq")
            jobs("e_nk")
            jobs("e_nv")
            pe.wait_ge(job_evac, evacuated("e_out"))
            pe.wait_ge(R["bias_ready"], 3)
            attention(T_N, len(T_A) + len(T_B), 10, MIX["hg"])
            pe.wait_ge(R["mix_lo_done"], MIX["na"])
            jobs("e_out")
            stat()
            ffn("ffn2", 2)

            stat()
            jobs("o_b", fresh=True)
            jobs("o_cu")
            pe.wait_ge(R["mix_lo_done"], MIX["od"])
            jobs("o_out")
            stat()
            ffn("ffn3", 3, ada=False)
            stat()


def kernel(**inputs):
    import numpy as np
    import concourse.bacc as bacc
    from concourse.bass_utils import run_bass_kernel_spmd as run

    a = {k: np.asarray(v) for k, v in inputs.items()}

    def rows(m):
        return np.ascontiguousarray(m.T.reshape(KB, P, -1).transpose(1, 0, 2))

    def cols(v):
        v = v.reshape(v.shape[:-1] + (-1, P))
        return np.moveaxis(v, -1, 0)

    def units(w):
        n = w.shape[1] // 256
        return w.reshape(KB, P, n, 256).transpose(2, 1, 0, 3).reshape(n, P, 2048)

    def ffn_units(first, second, down):
        g, u = units(first), units(second)
        d = down.reshape(NI, 2, P, D).transpose(0, 2, 1, 3).reshape(NI, P, 2048)
        out = [g[0], u[0]]
        for i in range(1, NI):
            out += [g[i], u[i], d[i - 1]]
        return np.stack(out + [d[NI - 1]])

    wa, e, o = a["a_w_in"][0], a["ev_w_in_2"][0], a["od_w_in_2"][0]
    ev = [units(e[:, 512 * i:512 * i + 512]) for i in range(8)]
    oc, ou = units(o[:, D:2 * D]), units(o[:, 2 * D:])
    mem_kv = [units(a["mem_w_kv"][l]) for l in range(2)]
    up, up2 = a["ffn_w_up"], a["ffn_w_up_2"]
    stream = [
        mem_kv[0], mem_kv[1],
        units(wa[:, :3072]), units(wa[:, 3080:]), units(a["a_w_out"][0]),
        ffn_units(up[0][:, FF:], up[0][:, :FF], a["ffn_w_down"][0]),
        units(a["w_kv"]), units(a["b_w_in"][0]), units(a["b_w_out"][0]),
        ffn_units(up[1][:, FF:], up[1][:, :FF], a["ffn_w_down"][1]),
        ev[4], ev[5], ev[6], ev[3], ev[7], ev[0], ev[1], ev[2], units(a["ev_w_out_2"][0]),
        ffn_units(up2[0][:, :FF], up2[0][:, FF:], a["ffn_w_down_2"][0]),
        units(o[:, :D]), np.stack([oc, ou], 1).reshape(8, P, 2048), units(a["od_w_out_2"][0]),
        ffn_units(up2[1][:, :FF], up2[1][:, FF:], a["ffn_w_down_2"][1]),
    ]

    def taps(w, b, order):
        return np.concatenate([cols(w[list(order)]).transpose(0, 2, 1), cols(b)[:, :, None]], axis=2)

    CAUSAL, CENTRED = (2, 1, 0), (1, 0, 2)
    ffn_taps = [taps(a["ffn_conv_w"][l], a["ffn_conv_b"][l], CAUSAL) for l in range(2)] + \
               [taps(a["ffn_conv_w_2"][l], a["ffn_conv_b_2"][l], CENTRED) for l in range(2)]
    parts = {
        "mix_g": cols(a["norm_mix_g"]), "ffn_g": cols(a["norm_ffn_g"]), "kv_g": cols(a["kv_norm_g"]),
        "fin_g": cols(a["final_g"]), "mix_w2": cols(a["norm_mix_w_2"]), "ffn_w2": cols(a["norm_ffn_w_2"]),
        "fin_w2": cols(a["final_norm_w_2"]),
        "a_conv": taps(a["a_conv_w"][0], a["a_conv_b"][0], (3, 2, 1, 0)),
        "a_head": cols(a["a_head_g"][0]),
        "ffn_conv": np.stack(ffn_taps, 1),
        "od_conv": taps(a["od_conv_w_2"][0], a["od_conv_b_2"][0], CENTRED),
        "ada_b": cols(a["ada_b_2"]), "hg_lb": cols(a["hg_lb_logits_2"]), "hg_w": cols(a["hg_norm_w_2"][0]),
        "cc": cols(np.stack([a["c_2"][0], a["c_ctx_2"]])).transpose(0, 2, 1),
        "gate_b": np.broadcast_to(a["a_gate_b"][0], (P, 8)),
    }
    vecs = np.concatenate([parts[n].reshape(P, -1) for n in VECS], axis=1)

    i = np.arange(P)
    q, k = i[:, None], i[None, :]
    same = (q // CH) == (k // CH)
    f32 = np.float32
    scan_f, scan_b = np.ones((P, 512), f32), np.ones((P, 512), f32)
    scan_f[:, 0:T:CH] = 0
    scan_f[:, T] = 0
    scan_b[:, CH - 1:T:CH] = 0
    scan_b[:, 511] = 0
    c = i % 64
    start = np.clip(c - 8, 0, 48)[:, None]
    cc = np.arange(64)[None, :]
    consts = {
        "ident": np.eye(P, dtype=f32), "flip": np.eye(P, dtype=f32)[::-1], "causal": (q <= k).astype(f32),
        "m_f": np.tile((same & (q <= k)).astype(f32), (1, 2)), "m_b": np.tile((same & (q >= k)).astype(f32), (1, 2)),
        "scan_f": scan_f, "scan_b": scan_b, "row4": (i[:, None] // CH == np.arange(4)[None]).astype(f32),
        "na": np.where((cc >= start) & (cc < start + 16), 0, NEG).astype(f32)[::-1],
    }
    cons = np.concatenate([consts[n] for n in CONS], axis=1)
    hcons = np.concatenate([consts[n] for n in HCONS], axis=1)

    relx = np.pad(a["b_rel_bias"][0][:, ::-1], ((0, 0), (127, 193)), mode="edge")
    nax = np.pad(a["na_rpb_2"][0][:, 4:11, :], ((0, 0), (0, 0), (48, 48)))

    arrays = {
        "x": rows(a["x"][0]), "mem": rows(a["mem"][0]), "ctx": rows(a["ctx_2"][0]),
        "vecs": vecs, "cons": cons, "gate": wa[:, 3072:3080].reshape(KB, P, 8).transpose(1, 0, 2),
        "units": np.concatenate(stream), "ada": np.concatenate([units(a["ada_w_2"][l]) for l in range(2)]),
        "hcons": hcons, "relx": relx, "nax": nax,
    }
    nc = bacc.Bacc("TRN2", target_bir_lowering=False, num_devices=1)
    io = {}
    for n in arrays:
        arrays[n] = np.ascontiguousarray(arrays[n])
        io[n] = nc.dram_tensor(f"in_{n}", arrays[n].shape, FP, kind="ExternalInput").ap()
    out = nc.dram_tensor("out_0", (P, KB, T), FP, kind="ExternalOutput").ap()
    build(nc, io, out)
    r = run(nc, [{f"in_{n}": v for n, v in arrays.items()}], core_ids=[0])
    got = r.results[0]["out_0"]
    return got.transpose(2, 1, 0).reshape(1, T, D)
```

```python
import concourse.bass as bass
from concourse import mybir
from contextlib import ExitStack

FP = mybir.dt.float32
FR = mybir.dt.float32r
U32 = mybir.dt.uint32
ACT = mybir.ActivationFunctionType
ALU = mybir.AluOpType
AXX = mybir.AxisListType.X

P = 128
D = 1024
KB = D // P
T = 256
EPS = 1e-6
FF = 2816
NI = FF // 256
RING = 3
NEG = -1e30
MH, MD = 4, 192
BH = 12
HGH = 4
CH = 32
NCH = T // CH

STREAM = [
    ("mk0", 1, "fm", "ctx"), ("mv0", 1, "tm", "ctx"), ("mk1", 1, "fm", "ctx"), ("mv1", 1, "tm", "ctx"),
    ("a_qk", 6, "fm", "lat"), ("a_v", 3, "tm", "lat"), ("a_o", 3, "fm", "lat"), ("a_qm", 1, "fm", "lat"),
    ("ada_a", 8, "ada", None), ("a_out", 4, "fm", "mix"), ("ffn0", 3 * NI, "ffn", "lat"),
    ("kv_k", 3, "fm", "lat"), ("kv_v", 3, "tm", "lat"), ("b_q", 3, "fm", "lat"), ("b_qm", 1, "fm", "lat"),
    ("ada_b", 16, "ada", None), ("b_out", 4, "fm", "mix"), ("ffn1", 3 * NI, "ffn", "lat"),
    ("e_ff", 2, "fm2", "both"), ("e_fb", 2, "fm2", "both"), ("e_hi", 2, "tm2", "both"),
    ("e_hq", 2, "fm", "lat"), ("e_hg", 2, "fm", "lat"), ("ada_h", 24, "ada", None),
    ("e_nq", 2, "fm", "lat"), ("e_nk", 2, "fm2", "both"), ("e_nv", 2, "tm2", "both"),
    ("e_out", 4, "fm", "mix"), ("ffn2", 3 * NI, "ffn", "lat"),
    ("o_b", 4, "fm", "lat"), ("o_cu", 8, "fm", "lat"), ("o_out", 4, "fm", "mix"), ("ffn3", 3 * NI, "ffn", "lat"),
]


class Job:
    def __init__(self, unit, kind, half, src, number, banked):
        self.unit, self.kind, self.half, self.src = unit, kind, half, src
        self.number, self.banked = number, banked


def plan():
    jobs, unit, number, banked, last, ada, seen = {}, 0, 0, 0, [], {}, 0
    for name, units, kind, src in STREAM:
        out = []
        if kind == "ada":
            ada[name] = seen
            seen += units
        for u in range(units):
            for half in range(2 if kind.endswith("2") else 1):
                fills = kind != "ada" and not (kind == "ffn" and ffn_kind(u) == "down")
                out.append(Job(unit + u, kind, half, src, number, banked if fills else None))
                number += 1
                banked += fills
            last.append(number)
        jobs[name] = out
        unit += units
    return jobs, unit, last, ada


def ffn_kind(u):
    if u < 2:
        return ("g", "u")[u]
    return ("g", "u", "down")[(u - 2) % 3] if u < 3 * NI - 1 else "down"


JOBS, NU, LAST, ADA = plan()
MODS = [(n, j) for n in ADA for j in JOBS[n]]
ADA_UNITS = {j.unit for _, j in MODS}

VECS = {}
_at = 0
for _n, _w in [("mix_g", 16), ("ffn_g", 16), ("kv_g", 8), ("fin_g", 8), ("mix_w2", 16), ("ffn_w2", 16),
               ("fin_w2", 8), ("a_conv", 60), ("a_head", 6), ("ffn_conv", 4 * NI * 8), ("od_conv", 32),
               ("ada_b", 96), ("hg_lb", 16), ("hg_w", 4), ("cc", 16), ("gate_b", 8)]:
    VECS[_n] = (_at, _w)
    _at += _w
NVEC = _at
CONS = {}
_at = 0
for _n, _w in [("ident", 128), ("flip", 128), ("causal", 128), ("row4", 4), ("fold", 2), ("na", 64)]:
    CONS[_n] = (_at, _w)
    _at += _w
NCON = _at
HCONS = {"m_f": (0, T), "m_b": (T, T), "scan_f": (512, 512), "scan_b": (1024, 512)}



def build(nc, io, out):
    JN = JOBS
    with ExitStack() as ctx:
        def sb(name, shape, dt=FP):
            return ctx.enter_context(nc.sbuf_tensor(name, shape, dt))

        def sem(name):
            return ctx.enter_context(nc.semaphore(name))

        raw = [sb(f"raw{i}", [P, 2048]) for i in range(RING)]
        whi = [sb(f"whi{i}", [P, 2048], FR) for i in range(RING)]
        wlo = [sb(f"wlo{i}", [P, 2048], FR) for i in range(RING)]
        x = sb("x", [P, KB, T])
        t = sb("t", [P, KB, T])
        h_hi = sb("h_hi", [P, KB, 512], FR)
        h_lo = sb("h_lo", [P, KB, 512], FR)
        mix_hi = sb("mix_hi", [P, KB, T], FR)
        mix_lo = sb("mix_lo", [P, KB, T], FR)
        hd_hi = sb("hd_hi", [P, 2, T], FR)
        hd_lo = sb("hd_lo", [P, 2, T], FR)
        vec = sb("vec", [P, NVEC])
        con = sb("con", [P, NCON])
        ones = sb("ones", [P, T])
        gw = sb("gw", [P, KB, 8])
        lb = sb("lb", [P, 4, 2, HGH])
        rs = sb("rs", [P, T])
        var = sb("var", [P, T])
        sc = sb("sc", [P, KB, 2])
        sc_hl = sb("sc_hl", [P, KB, 4], FR)
        mod = sb("mod", [P, 2, 48, 2])
        gain = sb("gain", [P, 5, KB])
        arena_floats = 14976
        arena = sb("arena", [P, arena_floats])

        def area(at, *shape):
            n = 1
            for s in shape:
                n *= s
            assert at + n <= arena_floats, (at, n)
            a = arena[:, at:at + n]
            if len(shape) == 1:
                return a
            if len(shape) == 2:
                return a.rearrange("p (a b) -> p a b", b=shape[1])
            return a.rearrange("p (a b c) -> p a b c", b=shape[1], c=shape[2])

        def idle(at, *shape):
            a = t[:].rearrange("p k n -> p (k n)")[:, at:at + (shape[0] * shape[1] if len(shape) > 1 else shape[0])]
            return a.rearrange("p (a b) -> p a b", b=shape[1]) if len(shape) > 1 else a

        g_row = idle(0, 6, T)
        b_p = [idle(256 * i, 256) for i in range(3)]
        b_t = [idle(768 + 256 * i, 256) for i in range(2)]
        s_am = [idle(1536, T), idle(1792, T)]
        small = [sb(f"small{i}", [P, 4]) for i in range(3)]
        s_dec = [sb(f"s_dec{i}", [P, NCH]) for i in range(2)]

        mkv = area(0, 2, 2, 512)
        sq = area(arena_floats - KB * T, KB, T)
        aq = area(2048, 6, T)
        ak = area(3584, 6, T)
        av = area(5120, 2, 768)
        ao = area(6656, 6, T)
        qm = area(8192, 2, T)
        m_arg = area(8704, 384)
        m_e = area(9088, 384)
        m_p = area(9472, 384)
        m_em = [area(9856, T), area(10112, T)]
        m_d = area(10368, T)
        m_d2 = area(10624, T)
        m_sq = area(10880, 2, T)
        m_v = area(11392, MH, T)
        m_y = [m_sq, area(11392, 2, T)]
        m_hm = aq
        g_tm = area(12416, 2, 8)
        g_col = area(12432, 2, 4)
        m_sel = area(12440, 4, P)
        f_y = area(8704, 2, T)
        f_s = area(9216, 2, T)
        f_h = area(9728, 2, T)
        bk = area(2048, 6, T)
        bv = area(3584, 2, 768)
        bq = area(5120, 6, T)
        bqm = area(6656, 2, T)
        band = area(7168, BH, 384)
        ctxx = area(0, KB, T)
        hf = [area(0, HGH, 512), area(2048, HGH, 512)]
        hv = area(4096, 4, 512)
        hq = area(6144, HGH, T)
        hg = area(7168, HGH, T)
        s_fg = [area(8192 + 512 * i, 512) for i in range(2)]
        s_b = [area(9216 + 512 * i, 512) for i in range(2)]
        s_bd = [area(10240 + 512 * i, 512) for i in range(2)]
        s_q = [area(11264 + T * i, T) for i in range(2)]
        s_k = [area(11776 + T * i, T) for i in range(2)]
        s_kt = area(12288, 4, P)
        s_st = area(12800, NCH, P)
        s_vb = area(13824, 2, 512)
        nbias = area(0, 48, 64)
        nq = area(3072, 4, T)
        nk = area(4096, 4, 512)
        nv = area(6144, 4, 512)
        n_p = [area(8192 + 512 * i, 512) for i in range(3)]
        n_t = [area(9728 + 512 * i, 512) for i in range(2)]
        ogb = area(0, KB, T)
        ogc = area(2048, 2, T)
        ocu = area(2560, 2, T)
        ocv = area(3072, 2, T)

        def vc(name, c=0, n=1):
            at = VECS[name][0] + c
            return vec[:, at:at + n]

        def cn(name):
            if name in HCONS:
                return idle(*HCONS[name])
            at, w = CONS[name]
            return con[:, at:at + w]

        def psum(name):
            return ctx.enter_context(nc.psum_tensor(name, [P, 512], FP))

        L = [psum("L0"), psum("L1")]
        Dn = [psum(f"D{i}") for i in range(4)]
        M0 = psum("M0")
        N0 = psum("N0")
        ident = cn("ident")
        m_rows = M0[0:4, T:512]
        spare = area(12960, 2 * P)
        ada_row = {n: (spare[0:4, 0:P], spare[0:4, P:2 * P]) for n in ("ada_a", "ada_b")}
        ada_row["ada_h"] = (area(14848, P)[0:4], cn("causal")[0:4])
        m_cols = M0[:, 0:192].rearrange("p (a b) -> p a b", b=2)

        def tile(h, qb, q, k, w, v, mix, bufs, bias=None, nb=0):
            pr = (h % 2) * 64
            return dict(w=w, pr=pr, qb=qb, mix=mix + h // 2, bias=bias, nb=nb, v=v, p=bufs[0],
                        t=bufs[1], q=q[pr:pr + 64, h // 2, qb * P:qb * P + P], k=k(slice(pr, pr + 64), h // 2, w))

        def memory_tiles(layer, q):
            return [tile(h, qb, q, lambda p, c, w: mkv[p, layer, 0, c * T:c * T + w], T,
                         [mkv[:, layer, 1, kb * 256 + h * 64:kb * 256 + h * 64 + 64] for kb in range(2)],
                         6, (b_p, b_t)) for h in range(4) for qb in range(2)]

        T_A = memory_tiles(0, qm)
        T_B = [tile(h, qb, bq, lambda p, c, w: bk[p, c, 0:w], P * (qb + 1),
                    [bv[:, kb, h * 64:h * 64 + 64] for kb in range(qb + 1)], 0, (b_p, b_t),
                    band[:, h, P * qb:P * qb + P * (qb + 1)], P * (qb + 1))
               for h in range(BH) for qb in range(2)] + memory_tiles(1, bqm)
        T_N = [tile(h, qb, nq, lambda p, c, w: nk[p, c, 0:w], 512,
                    [nv[:, kb, h * 64:h * 64 + 64] for kb in range(4)], 0, (n_p, n_t),
                    nbias[:, h * 6 + 2 - 2 * qb:h * 6 + 6 - 2 * qb, :].rearrange("p a b -> p (a b)"), T)
               for h in range(8) for qb in range(2)]
        SB_, PT_, OB = [Dn[0], Dn[1], L[1]], [Dn[2], Dn[3]], [N0, L[0]]

        ld = {n: sem(f"ld_{n}") for n in ("x", "mem", "vec", "con", "gate", "ctx", "band", "nbias", "hcons")}
        raw_full = [sem(f"raw_full{i}") for i in range(RING)]
        unit_hi, unit_lo = sem("unit_hi"), sem("unit_lo")
        job_done, job_evac = sem("job_done"), sem("job_evac")
        out_done = sem("out_done")
        dve_step, act_step = sem("dve_step"), sem("act_step")
        R = {n: sem(n) for n in (
            "ones_set", "cc_ready", "sc_hi", "sc_lo", "ada_out", "ada_turned", "ctx_hi", "ctx_lo", "sq_done", "ss_done", "rv_done", "rs_done", "t_done",
            "h_hi_done", "h_lo_done", "x_ready", "mod_ready", "q_silu", "o_sig",
            "gate_tm", "gate_sum", "gate_T", "gate_in", "gate_e", "gate_l", "row_ready", "em_exp", "em_ready",
            "acol_T", "acol_ready", "ml_s", "ml_arg", "ml_e", "ml_mask", "ml_p", "ml_num", "ml_sq", "ml_ss",
            "ml_post", "ml_rv", "ml_rs", "ml_h", "mix_hi_done", "mix_lo_done", "ffn_act", "hdh_done", "hdl_done", "down_done",
            "at_sc", "at_max", "at_exp", "at_nrm", "at_tp", "at_pt", "at_o", "bias_ready", "hgf_sig", "hgq_silu",
            "lb_in", "lb_exp", "hg_fg", "hg_g", "hg_b", "hg_bd", "hg_e", "hg_kd", "hg_vb", "hg_att", "hg_kdt",
            "hg_am", "hg_u", "hg_st", "hg_o", "hg_sq", "hg_ss", "hg_rv", "hg_rs", "hg_h", "od_h")}

        MIX = {"ml": 2, "memA": 4, "B": 12, "hg": 16, "na": 20, "od": 24}
        N_FINAL = 11

        def pieces(h):
            b = 3 * (h // 2)
            return (b, b + 1, 0) if h % 2 == 0 else (b + 2, b + 1, 64)

        def evacuated(name):
            j = JOBS[name][0]
            return j.banked

        def finished(name):
            return JOBS[name][-1].number + 1

        block = ctx.enter_context(nc.Block())

        @block.sync
        def _(sp):
            for v in range(RING):
                sp.dma_start(raw[v][:], io["units"][v]).then_inc(raw_full[v], 16)
            whole = NU // RING
            with sp.Fori(1, whole) as g:
                for r in range(RING):
                    sp.wait_ge(unit_lo, RING * g + (r + 1 - RING))
                    sp.dma_start(raw[r][:], io["units"][bass.ds(RING * g + r, 1)].rearrange("a p n -> (a p) n")) \
                        .then_inc(raw_full[r], 16)
            for v in range(whole * RING, NU):
                sp.wait_ge(unit_lo, v - RING + 1)
                sp.dma_start(raw[v % RING][:], io["units"][v]).then_inc(raw_full[v % RING], 16)
            for k in range(KB):
                sp.wait_ge(R["t_done"], KB * N_FINAL + k + 1)
                sp.dma_start(out[:, k, :], t[:, k, :]).then_inc(out_done, 16)
            sp.wait_ge(out_done, 16 * KB)

        @block.gpsimd
        def _(gp):
            def windows(ap, pattern):
                return bass.AP(tensor=ap.tensor, offset=ap.offset, ap=pattern)

            def lo(j):
                v = j.unit
                gp.wait_ge(unit_hi, v + 1)
                gp.wait_ge(unit_lo, v)
                nc.gpsimd.tensor_tensor(wlo[v % RING][:], raw[v % RING][:], whi[v % RING][:].bitcast(FP),
                                        ALU.subtract).then_inc(unit_lo, 1)

            nc.gpsimd.memset(ones[:], 1.0).then_inc(R["ones_set"], 1)
            gp.wait_ge(ld["con"], 16)
            for h in range(MH):
                gp.wait_ge(R["ml_e"], h + 1)
                for c in (0, T):
                    nc.gpsimd.tensor_tensor(m_e[:, c:c + P], m_e[:, c:c + P], cn("causal"), ALU.mult) \
                        .then_inc(R["ml_mask"], 1)
                for j in JOBS["ada_a"][2 * h:2 * h + 2]:
                    lo(j)
            gp.wait_ge(R["rs_done"], 3)
            for h in range(BH):
                for qb in range(2):
                    w = P * (qb + 1)
                    gp.dma_start(band[:, h, P * qb:P * qb + w],
                                 windows(io["relx"][h, P * (1 - qb):256], [[1, P], [1, w]])) \
                        .then_inc(ld["band"], 16)
            for j in JOBS["ada_b"]:
                lo(j)
            gp.wait_ge(R["hdl_done"], 2 * NI)
            gp.dma_start(ctxx, io["ctx"]).then_inc(ld["ctx"], 16)
            gp.wait_ge(R["h_lo_done"], KB * 7)
            gp.dma_start(t[:].rearrange("p k n -> p (k n)")[:, 0:1536], io["hcons"]).then_inc(ld["hcons"], 16)
            for j in JOBS["ada_h"]:
                lo(j)
            gp.wait_ge(R["mix_lo_done"], MIX["hg"])
            for half in range(2):
                for h in range(8):
                    gp.dma_start(nbias[64 - 64 * half:128 - 64 * half, 6 * h:6 * h + 6, :],
                                 windows(io["nax"][h, 1 - half, 0:64], [[1, 64], [127, 6], [1, 64]])) \
                        .then_inc(ld["nbias"], 16)

        @block.scalar
        def _(act):
            A = nc.scalar
            made, stats, applied, copied = [0], [0], [0], [0]

            def hi(v):
                act.wait_ge(raw_full[v % RING], 16 * (v // RING + 1))
                if v >= RING:
                    act.wait_ge(job_done, LAST[v - RING])
                A.activation(whi[v % RING][:], raw[v % RING][:], ACT.Copy).then_inc(unit_hi, 1)

            def rows_out():
                name, j = MODS[copied[0]]
                act.wait_ge(job_done, j.number + 1)
                if ADA[name] != copied[0]:
                    act.wait_ge(R["ada_turned"], copied[0])
                for c in range(2):
                    A.activation(ada_row[name][c], m_rows[:, c * P:c * P + P], ACT.Copy) \
                        .then_inc(R["ada_out"], 1)
                copied[0] += 1

            def upto(v):
                while made[0] <= min(v, NU - 1):
                    if copied[0] < len(MODS) and made[0] - RING == MODS[copied[0]][1].unit:
                        rows_out()
                    hi(made[0])
                    made[0] += 1

            def jobs(name, after=None):
                for n, j in enumerate(JOBS[name]):
                    upto(j.unit + 2)
                    if after:
                        act.wait_ge(job_evac, j.banked + 1)
                        after(n, j)

            def square(src, i):
                A.activation(sq[:, 2 * i:2 * i + 2, :], src[:, 2 * i:2 * i + 2, :], ACT.Square) \
                    .then_inc(R["sq_done"], 1)

            def root():
                stats[0] += 1
                act.wait_ge(R["rv_done"], stats[0])
                A.activation(rs[:], var[:], ACT.Sqrt).then_inc(R["rs_done"], 1)

            def stat(src, ready):
                for i in range(4):
                    act.wait_ge(*ready(i))
                    square(src, i)
                root()

            def apply(shift=None, col=0, before=None):
                base = KB * applied[0]
                applied[0] += 1
                if before:
                    act.wait_ge(job_done, before)
                for k in range(KB):
                    act.wait_ge(R["t_done"], base + k + 1)
                    dst = h_hi[:, k, col:col + T]
                    if shift is None:
                        A.activation(dst, t[:, k, :], ACT.Copy).then_inc(R["h_hi_done"], 1)
                    else:
                        A.activation(dst, t[:, k, :], ACT.Identity, bias=shift(k)).then_inc(R["h_hi_done"], 1)

            def ffn_parts(n):
                return lambda i: (R["x_ready"], 4 * n + i + 1)

            def attention(tl, t0, g0, ahead=False):
                n = len(tl)
                for i in range(n + 5):
                    if i < n:
                        a, g = tl[i], t0 + i
                        act.wait_ge(R["at_max"], g + 1)
                        if g >= 3:
                            act.wait_ge(R["at_tp"], g - 2)
                        A.activation(a["p"][g % 3][:, 0:a["w"]], SB_[g % 3][:, 0:a["w"]], ACT.Exp,
                                     bias=small[g % 3][:, 0:1], accum_out=small[g % 3][:, 1:2]) \
                            .then_inc(R["at_exp"], 1)
                    if 0 <= i - 2 < n:
                        a, g = tl[i - 2], t0 + i - 2
                        act.wait_ge(R["at_tp"], g + 1)
                        if g >= 2:
                            act.wait_ge(R["at_o"], g - 1)
                        A.activation(a["t"][g % 2][:, 0:a["w"]], PT_[g % 2][:, 0:a["w"]], ACT.Copy) \
                            .then_inc(R["at_pt"], 1)
                    if i >= 4 and (i - 4) % 4 == 3:
                        gg = (i - 4) // 4
                        act.wait_ge(R["at_o"], t0 + i - 3)
                        A.activation(mix_hi[:, tl[i - 4]["mix"], :], OB[(g0 + gg) % 2][:, 0:T], ACT.Copy) \
                            .then_inc(R["mix_hi_done"], 1)
                    if ahead and i < n and i % 2:
                        rows_out()
                        upto(made[0])

            def ffn(name, f, func):
                j0, u0, b0 = JOBS[name][0].number, JOBS[name][0].unit, JOBS[name][0].banked

                def wh(r, i):
                    s = (u0 + r) % RING
                    act.wait_ge(raw_full[s], i * 16 + 16 * ((u0 + r) // RING + 1))
                    act.wait_ge(job_done, i * 3 + (j0 + r - RING + 1))
                    A.activation(whi[s][:], raw[s][:], ACT.Copy).then_inc(unit_hi, 1)

                def gate(i):
                    act.wait_ge(job_evac, i * 2 + (b0 + 1))
                    A.activation(f_s, f_y, func).then_inc(R["ffn_act"], 1)

                def hidden(i, down):
                    act.wait_ge(job_evac, i * 2 + (b0 + 2))
                    if down is not None:
                        act.wait_ge(job_done, down)
                    A.activation(hd_hi[:], f_h, ACT.Copy).then_inc(R["hdh_done"], 1)

                upto(u0 + 2)
                gate(0)
                upto(u0 + 3)
                hidden(0, None)
                upto(u0 + 4)
                gate(1)
                upto(u0 + 5)
                upto(u0 + 6)
                hidden(1, j0 + 5)
                with act.Fori(2, NI - 1) as i:
                    wh(1, i)
                    gate(i)
                    wh(2, i)
                    wh(3, i)
                    hidden(i, i * 3 + (j0 + 2))
                made[0] = u0 + 3 * (NI - 1) + 1
                i = NI - 1
                upto(u0 + 3 * i + 1)
                gate(i)
                upto(u0 + 3 * i + 2)
                upto(u0 + 3 * i + 3)
                hidden(i, i * 3 + (j0 + 2))

            act.dma_start(t[:], io["mem"]).then_inc(ld["mem"], 16)
            act.dma_start(x[:], io["x"]).then_inc(ld["x"], 16)
            act.dma_start(vec[:], io["vecs"]).then_inc(ld["vec"], 16)
            act.dma_start(gw[:], io["gate"]).then_inc(ld["gate"], 16)
            act.dma_start(con[:], io["cons"]).then_inc(ld["con"], 16)

            act.wait_ge(ld["mem"], 16)
            A.activation(h_hi[:, :, T:512], t[:], ACT.Copy).then_inc(R["ctx_hi"], 1)
            upto(1)
            act.wait_ge(ld["x"], 16)
            for i in range(4):
                square(x, i)
            act.wait_ge(ld["vec"], 16)
            A.activation(sc[:].rearrange("p k n -> p (k n)"), vc("cc", 0, 16), ACT.Silu).then_inc(R["cc_ready"], 1)
            act.wait_ge(R["cc_ready"], 1)
            A.activation(sc_hl[:, :, 0:2], sc[:], ACT.Copy).then_inc(R["sc_hi"], 1)
            jobs("mk0")
            root()
            jobs("mv0")
            apply()
            jobs("mk1")
            jobs("mv1")

            def q_silu(n, j):
                dst = (aq if n < 3 else ak)[:, 2 * (n % 3):2 * (n % 3) + 2, :]
                A.activation(dst, m_y[n % 2], ACT.Silu).then_inc(R["q_silu"], 1)

            def o_sig(n, j):
                dst = ao[:, 2 * n:2 * n + 2, :]
                A.activation(dst, dst, ACT.Sigmoid).then_inc(R["o_sig"], 1)

            jobs("a_qk", q_silu)
            act.wait_ge(R["gate_in"], 1)
            A.activation(g_row[0:4, 2, :], g_row[0:4, 2, :], ACT.Exp).then_inc(R["gate_e"], 1)
            act.wait_ge(R["gate_e"], 1)
            A.activation(g_row[0:4, 2, :], g_row[0:4, 2, :], ACT.Ln, bias=1.0).then_inc(R["gate_l"], 1)
            jobs("a_v")
            act.wait_ge(R["row_ready"], 1)
            A.activation(g_row[0:4, 5, :], g_row[0:4, 5, :], ACT.Exp, scale=-1.0).then_inc(R["em_exp"], 1)
            jobs("a_o", o_sig)
            jobs("a_qm")
            for h in range(MH + 1):
                if h < MH:
                    act.wait_ge(R["ml_arg"], h + 1)
                    if h:
                        act.wait_ge(R["ml_p"], h)
                    A.activation(m_e, m_arg, ACT.Exp).then_inc(R["ml_e"], 1)
                if h:
                    _, _, pr = pieces(h - 1)
                    act.wait_ge(R["ml_num"], h)
                    if h > 1:
                        act.wait_ge(R["ml_ss"], h - 1)
                    A.activation(m_sq[:, 0, :], Dn[2][:, 0:T], ACT.Square).then_inc(R["ml_sq"], 1)
                    A.activation(m_sq[pr:pr + 64, 1, :], Dn[2][pr:pr + 64, T:512], ACT.Square) \
                        .then_inc(R["ml_sq"], 1)
                upto(JOBS["ada_a"][0].unit + 2 * h + 1)
            rows_out()
            act.wait_ge(R["ml_rv"], MH)
            A.activation(m_v, m_v, ACT.Sqrt).then_inc(R["ml_rs"], 1)
            for i in range(2):
                act.wait_ge(R["ml_h"], 4 * i + 4)
                A.activation(mix_hi[:, 3 * i:3 * i + 3, :], m_hm[:, 3 * i:3 * i + 3, :], ACT.Copy) \
                    .then_inc(R["mix_hi_done"], 1)
            attention(T_A, 0, 0)
            jobs("a_out", lambda n, j: square(x, n))
            root()
            apply()
            ffn("ffn0", 0, ACT.Silu)

            stat(x, ffn_parts(0))
            apply(before=finished("ffn0"))
            jobs("kv_k")
            jobs("kv_v")
            apply(before=finished("kv_v"))
            jobs("b_q")
            jobs("b_qm")
            attention(T_B, len(T_A), 2, ahead=True)
            jobs("b_out", lambda n, j: square(x, n))
            root()
            apply()
            ffn("ffn1", 1, ACT.Silu)

            stat(x, ffn_parts(1))
            applied[0] += 1
            stat(ctxx, lambda i: (ld["ctx"], 16))
            act.wait_ge(R["mod_ready"], 1)
            apply(lambda k: mod[:, 0, k, 1:2], T)
            stat(x, lambda i: (R["t_done"], KB * 5 + 2 * i + 2))
            apply(lambda k: mod[:, 0, k, 0:1])

            def f_sig(d):
                def run(n, j):
                    A.activation(hf[d][:, n, :], hf[d][:, n, :], ACT.Sigmoid).then_inc(R["hgf_sig"], 1)
                return run

            def hq_silu(dst):
                def run(n, j):
                    A.activation(dst[:, 2 * n:2 * n + 2, :], dst[:, 2 * n:2 * n + 2, :], ACT.Silu) \
                        .then_inc(R["hgq_silu"], 1)
                return run

            jobs("e_ff", f_sig(0))
            jobs("e_fb", f_sig(1))
            jobs("e_hi")
            jobs("e_hq", hq_silu(hq))
            jobs("e_hg", hq_silu(hg))
            act.wait_ge(R["lb_in"], 1)
            A.activation(lb[:, 0:2], lb[:, 0:2], ACT.Exp).then_inc(R["lb_exp"], 1)
            ada0 = JOBS["ada_h"][0].unit
            for e in range(2 * HGH + 2):
                s = e % 2
                if e < 2 * HGH:
                    act.wait_ge(R["hg_fg"], e + 1)
                    A.activation(s_b[s], s_fg[s], ACT.Ln).then_inc(R["hg_g"], 1)
                if 0 < e <= 2 * HGH:
                    act.wait_ge(R["hg_att"], e)
                    A.activation(s_kt.rearrange("p a b -> p (a b)"), Dn[1][:], ACT.Copy).then_inc(R["hg_kdt"], 1)
                if 0 < e <= 2 * HGH:
                    upto(ada0 + 3 * e - 1)
                if e < 2 * HGH:
                    act.wait_ge(R["hg_b"], e + 1)
                    if e > 1:
                        act.wait_ge(R["hg_o"], e - 1)
                    A.activation(s_q[s], s_b[s][:, 0:T], ACT.Exp).then_inc(R["hg_e"], 1)
                    A.activation(s_k[s], s_b[s][:, 0:T], ACT.Exp, scale=-1.0).then_inc(R["hg_e"], 1)
                    ends = s_b[s][:, CH - 1:T:CH] if s == 0 else s_b[s][:, 0:T:CH]
                    A.activation(s_dec[s][:], ends, ACT.Exp).then_inc(R["hg_e"], 1)
                    act.wait_ge(R["hg_bd"], e + 1)
                    A.activation(s_bd[s], s_bd[s], ACT.Exp).then_inc(R["hg_e"], 1)
                if 0 < e <= 2 * HGH:
                    upto(ada0 + 3 * e)
                    upto(ada0 + 3 * e + 1)
                if e >= 2 and e % 2 == 0:
                    h = e // 2 - 1
                    act.wait_ge(R["hg_o"], e)
                    A.activation(hf[0][:, h, 0:T], L[h % 2][:, 0:T], ACT.Square).then_inc(R["hg_sq"], 1)
                if e >= 3 and e % 2 == 1:
                    h = (e - 3) // 2
                    act.wait_ge(R["hg_rv"], h + 1)
                    A.activation(rs[:], var[:], ACT.Sqrt).then_inc(R["hg_rs"], 1)
                    act.wait_ge(R["hg_h"], h + 1)
                    A.activation(mix_hi[:, 4 + h, :], hf[0][:, h, T:512], ACT.Copy).then_inc(R["mix_hi_done"], 1)
            rows_out()
            jobs("e_nq")
            jobs("e_nk")
            jobs("e_nv")
            attention(T_N, len(T_A) + len(T_B), 10)
            jobs("e_out", lambda n, j: square(x, n))
            root()
            apply(lambda k: mod[:, 0, 24 + k, 0:1])
            ffn("ffn2", 2, ACT.Gelu)

            stat(x, ffn_parts(2))
            act.wait_ge(R["mod_ready"], 2)
            apply(lambda k: mod[:, 1, k, 0:1])
            jobs("o_b")

            def o_round(n, j):
                if n % 2:
                    act.wait_ge(R["od_h"], n // 2 + 1)
                    A.activation(mix_hi[:, n - 1:n + 1, :], ocv, ACT.Copy).then_inc(R["mix_hi_done"], 1)

            jobs("o_cu", o_round)
            jobs("o_out", lambda n, j: square(x, n))
            root()
            apply(lambda k: mod[:, 1, 24 + k, 0:1])
            ffn("ffn3", 3, ACT.Gelu)
            stat(x, ffn_parts(3))

        @block.vector
        def _(dve):
            V = nc.vector
            steps, made, stats, applied, rounded = [0], [0], [0], [0], [0]

            def step(ins):
                ins.then_inc(dve_step, 1)
                steps[0] = steps[0] + 1

            def sync():
                dve.wait_ge(dve_step, steps[0])

            def lo(v):
                dve.wait_ge(unit_hi, v + 1)
                V.tensor_tensor(wlo[v % RING][:], raw[v % RING][:], whi[v % RING][:].bitcast(FP), ALU.subtract) \
                    .then_inc(unit_lo, 1)

            def upto(v):
                while made[0] <= min(v, NU - 1) and made[0] not in ADA_UNITS:
                    lo(made[0])
                    made[0] += 1

            def past_ada(name):
                assert made[0] == JOBS[name][0].unit
                made[0] = JOBS[name][-1].unit + 1
                dve.wait_ge(unit_lo, made[0])
                upto(made[0] + 1)

            def bank(j):
                return L[j.banked % 2]

            def jobs(name, evac, after={}):
                for n, j in enumerate(JOBS[name]):
                    upto(j.unit + 2)
                    dve.wait_ge(job_done, j.number + 1)
                    evac(n, j, bank(j)).then_inc(job_evac, 1)
                    if n in after:
                        after[n]()

            def pair(ap):
                return ap.rearrange("p (a b) -> p a b", b=T)

            def stat(dim=D):
                dve.wait_ge(R["ss_done"], stats[0] + 1)
                stats[0] += 1
                step(V.tensor_scalar(var[:], N0[:, 0:T], 1.0 / dim, EPS, ALU.mult, ALU.add))
                sync()
                V.reciprocal(var[:], var[:]).then_inc(R["rv_done"], 1)

            def apply(g, src=None, dst=None, shift=None, col=0, before=None, to_h=True):
                src = x if src is None else src
                dst = t if dst is None else dst
                dve.wait_ge(R["rs_done"], stats[0])
                if before:
                    dve.wait_ge(job_done, before)
                for k in range(KB + 1):
                    if k < KB:
                        V.scalar_tensor_tensor(dst[:, k, :], src[:, k, :], g(k), rs[:], ALU.mult, ALU.mult) \
                            .then_inc(R["t_done"], 1)
                    if to_h and k:
                        q = k - 1
                        dve.wait_ge(R["h_hi_done"], rounded[0] + q + 1)
                        a, b = h_lo[:, q, col:col + T], h_hi[:, q, col:col + T].bitcast(FP)
                        if shift is None:
                            V.tensor_tensor(a, t[:, q, :], b, ALU.subtract).then_inc(R["h_lo_done"], 1)
                        else:
                            V.scalar_tensor_tensor(a, t[:, q, :], shift(q), b, ALU.add, ALU.subtract) \
                                .then_inc(R["h_lo_done"], 1)
                applied[0] += 1
                if to_h:
                    rounded[0] += KB

            def conv(y, src, taps, bias, offsets):
                for n, (w, o) in enumerate(zip(taps, offsets)):
                    for c in range(2):
                        if n == 0:
                            ins = V.tensor_scalar(y[:, c, :], src[:, c, :], w(c), bias(c), ALU.mult, ALU.add)
                        else:
                            a, b = (0, T - o) if o > 0 else (-o, T)
                            d = y[:, c, o:T] if o > 0 else y[:, c, 0:T + o]
                            ins = V.scalar_tensor_tensor(d, src[:, c, a:b], w(c), d, ALU.mult, ALU.add)
                        if n == len(taps) - 1 and c == 1:
                            return ins
                        step(ins)
                    sync()

            def attention(tl, t0, g0, mixbase, ada=None):
                n = len(tl)
                for i in range(n + 4):
                    if i < n:
                        a, g = tl[i], t0 + i
                        dve.wait_ge(R["at_sc"], g + 1)
                        V.tensor_reduce(small[g % 3][:, 0:1], SB_[g % 3][:, 0:a["w"]], AXX, ALU.max, negate=True) \
                            .then_inc(R["at_max"], 1)
                    if 0 <= i - 1 < n:
                        a, g = tl[i - 1], t0 + i - 1
                        dve.wait_ge(R["at_exp"], g + 1)
                        step(V.reciprocal(small[g % 3][:, 2:3], small[g % 3][:, 1:2]))
                        sync()
                        p = a["p"][g % 3][:, 0:a["w"]]
                        V.tensor_scalar(p, p, small[g % 3][:, 2:3], None, ALU.mult).then_inc(R["at_nrm"], 1)
                    if i >= 4 and (i - 4) % 4 == 3:
                        gg = (i - 4) // 4
                        m = tl[i - 4]["mix"]
                        dve.wait_ge(R["mix_hi_done"], mixbase + gg + 1)
                        V.tensor_tensor(mix_lo[:, m, :], OB[(g0 + gg) % 2][:, 0:T], mix_hi[:, m, :].bitcast(FP),
                                        ALU.subtract).then_inc(R["mix_lo_done"], 1)
                    if ada and i == n:
                        past_ada(ada)

            def residual(name, gate=None):
                def evac(n, j, b):
                    if gate is None:
                        dst = x[:, 2 * n:2 * n + 2, :]
                        return V.tensor_tensor(dst, dst, pair(b[:]), ALU.add)
                    d = [x[:, 2 * n + c, :] for c in range(2)]
                    step(V.scalar_tensor_tensor(d[0], b[:, 0:T], gate(2 * n), d[0], ALU.mult, ALU.add))
                    return V.scalar_tensor_tensor(d[1], b[:, T:512], gate(2 * n + 1), d[1], ALU.mult, ALU.add)
                jobs(name, evac)

            def ffn(name, f, offsets, gate=None):
                j0, u0, b0 = JOBS[name][0].number, JOBS[name][0].unit, JOBS[name][0].banked
                at = VECS["ffn_conv"][0] + 8 * NI * f
                g_bank, u_bank = L[b0 % 2], L[(b0 + 1) % 2]

                def wl(r, i):
                    s = (u0 + r) % RING
                    dve.wait_ge(unit_hi, i * 3 + (u0 + r + 1))
                    V.tensor_tensor(wlo[s][:], raw[s][:], whi[s][:].bitcast(FP), ALU.subtract).then_inc(unit_lo, 1)

                def tap(i, n):
                    def col(c):
                        o = i * 8 + (at + 4 * c + n)
                        return vec[:, o:o + 1] if isinstance(i, int) else vec[:, bass.ds(o, 1)]
                    return col

                def convolve(i, g_job):
                    dve.wait_ge(job_done, g_job + 1)
                    conv(f_y, pair(g_bank[:]), [tap(i, n) for n in range(3)], tap(i, 3), offsets) \
                        .then_inc(job_evac, 1)

                def multiply(i, u_job):
                    dve.wait_ge(job_done, u_job + 1)
                    dve.wait_ge(R["ffn_act"], i + (f * NI + 1))
                    V.tensor_tensor(f_h, f_s, pair(u_bank[:]), ALU.mult).then_inc(job_evac, 1)

                def hidden(i):
                    dve.wait_ge(R["hdh_done"], i + (f * NI + 1))
                    V.tensor_tensor(hd_lo[:], f_h, hd_hi[:].bitcast(FP), ALU.subtract).then_inc(R["hdl_done"], 1)

                upto(u0 + 2)
                convolve(0, j0)
                upto(u0 + 3)
                multiply(0, j0 + 1)
                hidden(0)
                upto(u0 + 4)
                convolve(1, j0 + 2)
                upto(u0 + 5)
                multiply(1, j0 + 3)
                upto(u0 + 6)
                hidden(1)
                n0 = steps[0]
                per = 5
                with dve.Fori(2, NI - 1) as i:
                    steps[0] = (i - 2) * per + n0
                    wl(1, i)
                    convolve(i, i * 3 + (j0 - 1))
                    wl(2, i)
                    multiply(i, i * 3 + j0)
                    wl(3, i)
                    hidden(i)
                steps[0] = n0 + per * (NI - 3)
                made[0] = u0 + 3 * (NI - 1) + 1
                i = NI - 1
                upto(u0 + 3 * i + 1)
                convolve(i, j0 + 3 * i - 1)
                upto(u0 + 3 * i + 2)
                multiply(i, j0 + 3 * i)
                upto(u0 + 3 * i + 3)
                hidden(i)
                for n in range(4):
                    if n < 3:
                        dve.wait_ge(R["down_done"], 3 * f + n + 1)
                    else:
                        dve.wait_ge(job_done, finished(name))
                    if gate is None:
                        dst = x[:, 2 * n:2 * n + 2, :]
                        V.tensor_tensor(dst, dst, pair(Dn[n][:]), ALU.add).then_inc(R["x_ready"], 1)
                    else:
                        for c in range(2):
                            dst = x[:, 2 * n + c, :]
                            ins = V.scalar_tensor_tensor(dst, Dn[n][:, c * T:c * T + T], gate(2 * n + c), dst,
                                                         ALU.mult, ALU.add)
                            if c:
                                ins.then_inc(R["x_ready"], 1)
                            else:
                                step(ins)

            CAUSAL3, CENTRED3 = (0, 1, 2), (0, 1, -1)

            dve.wait_ge(R["ctx_hi"], 1)
            V.tensor_tensor(h_lo[:, :, T:512], t[:], h_hi[:, :, T:512].bitcast(FP), ALU.subtract) \
                .then_inc(R["ctx_lo"], 1)
            upto(1)
            dve.wait_ge(R["sc_hi"], 1)
            V.tensor_tensor(sc_hl[:, :, 2:4], sc[:], sc_hl[:, :, 0:2].bitcast(FP), ALU.subtract) \
                .then_inc(R["sc_lo"], 1)

            def to_mkv(layer, which):
                return lambda n, j, b: V.tensor_copy(mkv[:, layer, which, :], b[:])

            jobs("mk0", to_mkv(0, 0))
            stat()
            jobs("mv0", to_mkv(0, 1))
            apply(lambda k: vc("mix_g", k))
            jobs("mk1", to_mkv(1, 0))
            jobs("mv1", to_mkv(1, 1))

            def qk_conv(n, j, b):
                if n >= 2:
                    dve.wait_ge(R["q_silu"], n - 1)
                at = VECS["a_conv"][0] + 10 * n
                return conv(m_y[n % 2], pair(b[:]),
                            [(lambda c, o=o: vec[:, at + 5 * c + o:at + 5 * c + o + 1]) for o in range(4)],
                            lambda c: vec[:, at + 5 * c + 4:at + 5 * c + 5], (0, 1, 2, 3))

            g4 = [g_row[0:4, i, :] for i in range(6)]

            def gate_bias():
                dve.wait_ge(R["gate_tm"], 1)
                V.tensor_tensor(g_tm, N0[:, 0:16].rearrange("p (a b) -> p a b", b=8),
                                vc("gate_b", 0, 8).unsqueeze(1).to_broadcast([P, 2, 8]), ALU.add) \
                    .then_inc(R["gate_sum"], 1)

            def gate_rows():
                dve.wait_ge(R["gate_T"], 1)
                step(V.tensor_copy(g_row[0:4, 0:2, :], N0[0:4, :].rearrange("p (a b) -> p a b", b=T)))
                sync()
                V.scalar_tensor_tensor(g4[2], g4[1], -1.0, g4[1], ALU.mult, ALU.min).then_inc(R["gate_in"], 1)
                step(V.tensor_scalar(g4[1], g4[1], 0.0, None, ALU.min))

            def gate_scans():
                dve.wait_ge(R["gate_l"], 1)
                sync()
                step(V.tensor_tensor(g4[1], g4[1], g4[2], ALU.subtract))
                sync()
                step(V.tensor_tensor_scan(g4[3], ones[0:4, :], g4[1], 0.0, ALU.mult, ALU.add))
                sync()
                step(V.tensor_tensor(g4[0], g4[0], g4[3], ALU.subtract))
                sync()
                step(V.tensor_tensor_scan(g4[4], g4[0], g4[0], 0.0, ALU.max, ALU.max))
                sync()
                step(V.tensor_tensor(g4[5], g4[3], g4[4], ALU.add))
                sync()
                V.tensor_scalar(g4[4], g4[4], -1.0, None, ALU.mult).then_inc(R["row_ready"], 1)

            def gate_columns():
                for h in range(MH):
                    step(V.tensor_copy(m_sel[0:4, h, :], ident[0:4, h:h + 1].to_broadcast([4, P])))
                dve.wait_ge(R["acol_T"], 1)
                step(V.tensor_copy(g_col.rearrange("p a b -> p (a b)"), N0[:, 0:8]))
                dve.wait_ge(R["em_exp"], 1)
                sync()
                V.tensor_scalar(g4[5], g4[5], 1e18, None, ALU.min).then_inc(R["em_ready"], 1)

            jobs("a_qk", qk_conv, {1: gate_bias, 5: gate_rows})
            jobs("a_v", lambda n, j, b: V.tensor_copy(av[:, :, 256 * n:256 * n + 256], pair(b[:])), {0: gate_scans})
            jobs("a_o", lambda n, j, b: V.tensor_copy(ao[:, 2 * n:2 * n + 2, :], pair(b[:])), {0: gate_columns})
            jobs("a_qm", lambda n, j, b: V.tensor_scalar(qm, pair(b[:]), 0.125, None, ALU.mult))

            def weight_logs(h):
                dve.wait_ge(R["ml_s"], h + 1)
                step(V.tensor_copy(m_em[h % 2], Dn[1][:, T:512]))
                step(V.tensor_scalar(m_arg[:, 0:T], Dn[1][:, 0:T], g_col[:, 0, h:h + 1], 0.0, ALU.add, ALU.min))
                V.tensor_scalar(m_arg[:, T:T + P], Dn[1][:, P:T], g_col[:, 1, h:h + 1], 0.0, ALU.add, ALU.min) \
                    .then_inc(R["ml_arg"], 1)

            def weigh(h):
                dve.wait_ge(R["ml_mask"], 2 * h + 2)
                V.scalar_tensor_tensor(m_p, Dn[0][:, 0:384], MD ** -0.5, m_e, ALU.mult, ALU.mult) \
                    .then_inc(R["ml_p"], 1)

            def numerator(h):
                full, half, pr = pieces(h)
                hp = slice(pr, pr + 64)
                dve.wait_ge(R["ml_num"], h + 1)
                sync()
                step(V.scalar_tensor_tensor(m_d, Dn[3][:, 0:T], -1.0, m_em[h % 2], ALU.mult, ALU.max))
                sync()
                step(V.scalar_tensor_tensor(m_d, Dn[3][:, 0:T], 1.0, m_d, ALU.mult, ALU.max))
                sync()
                step(V.scalar_tensor_tensor(m_d2, m_d, EPS, m_d, ALU.mult, ALU.mult))
                dve.wait_ge(R["ml_sq"], 2 * h + 2)
                step(V.scalar_tensor_tensor(ao[:, full, :], Dn[2][:, 0:T], vc("a_head", full), ao[:, full, :],
                                            ALU.mult, ALU.mult))
                step(V.scalar_tensor_tensor(ao[hp, half, :], Dn[2][hp, T:512], vc("a_head", half)[hp],
                                            ao[hp, half, :], ALU.mult, ALU.mult))

            def variance(h):
                dve.wait_ge(R["ml_ss"], h + 1)
                sync()
                V.scalar_tensor_tensor(m_v[:, h, :], N0[:, 0:T], 1.0 / MD, m_d2, ALU.mult, ALU.add) \
                    .then_inc(R["ml_post"], 1)
                dve.wait_ge(R["ml_post"], h + 1)
                step(V.tensor_scalar(m_v[:, h, :], m_v[:, h, :], 1e-34, 1e34, ALU.max, ALU.min))
                sync()
                V.reciprocal(m_v[:, h, :], m_v[:, h, :]).then_inc(R["ml_rv"], 1)

            dve.wait_ge(R["o_sig"], 3)
            weight_logs(0)
            weigh(0)
            for h in range(MH):
                if h + 1 < MH:
                    weight_logs(h + 1)
                numerator(h)
                if h + 1 < MH:
                    weigh(h + 1)
                variance(h)
            dve.wait_ge(R["ml_rs"], 1)
            for h in range(MH):
                full, half, pr = pieces(h)
                hp = slice(pr, pr + 64)
                V.tensor_tensor(m_hm[:, full, :], ao[:, full, :], m_v[:, h, :], ALU.mult).then_inc(R["ml_h"], 1)
                V.tensor_tensor(m_hm[hp, half, :], ao[hp, half, :], m_v[hp, h, :], ALU.mult).then_inc(R["ml_h"], 1)
            for i in range(2):
                b3 = slice(3 * i, 3 * i + 3)
                dve.wait_ge(R["ml_h"], 4 * i + 4)
                dve.wait_ge(R["mix_hi_done"], i + 1)
                V.tensor_tensor(mix_lo[:, b3, :], m_hm[:, b3, :], mix_hi[:, b3, :].bitcast(FP), ALU.subtract) \
                    .then_inc(R["mix_lo_done"], 1)
            attention(T_A, 0, 0, MIX["ml"], "ada_a")
            residual("a_out")
            stat()
            apply(lambda k: vc("ffn_g", k))
            ffn("ffn0", 0, CAUSAL3)

            stat()
            apply(lambda k: vc("kv_g", k), before=finished("ffn0"))
            jobs("kv_k", lambda n, j, b: V.tensor_copy(bk[:, 2 * n:2 * n + 2, :], pair(b[:])))
            jobs("kv_v", lambda n, j, b: V.tensor_copy(bv[:, :, 256 * n:256 * n + 256], pair(b[:])))
            apply(lambda k: vc("mix_g", KB + k), before=finished("kv_v"))
            jobs("b_q", lambda n, j, b: V.tensor_scalar(bq[:, 2 * n:2 * n + 2, :], pair(b[:]), 0.125, None, ALU.mult))
            jobs("b_qm", lambda n, j, b: V.tensor_scalar(bqm, pair(b[:]), 0.125, None, ALU.mult))
            dve.wait_ge(ld["band"], 16 * 2 * BH)
            V.memset(band[64:128, :, 64:128], NEG).then_inc(R["bias_ready"], 1)
            V.memset(band[64:128, :, P + 192:P + 256], NEG).then_inc(R["bias_ready"], 1)
            attention(T_B, len(T_A), 2, MIX["memA"], "ada_b")
            residual("b_out")
            stat()
            apply(lambda k: vc("ffn_g", KB + k))
            ffn("ffn1", 1, CAUSAL3)

            def modulation(layer, gains):
                dve.wait_ge(R["ada_turned"], 24 * (layer + 1))
                bias = vc("ada_b", 48 * layer, 48).unsqueeze(2).to_broadcast([P, 48, 2])
                step(V.tensor_tensor(mod[:, layer, :, :], m_cols[:, 48 * layer:48 * layer + 48, :], bias, ALU.add))
                sync()
                for n, (slot, blk, c, name, at) in enumerate(gains):
                    ins = V.scalar_tensor_tensor(gain[:, slot, :], mod[:, layer, blk:blk + KB, c], 1.0,
                                                 vc(name, at, KB), ALU.add, ALU.mult)
                    if n == len(gains) - 1:
                        ins.then_inc(R["mod_ready"], 1)
                    else:
                        step(ins)
                dve.wait_ge(R["mod_ready"], layer + 1)

            stat()
            apply(lambda k: vc("fin_g", k), dst=x, to_h=False)
            modulation(0, [(0, 8, 1, "mix_w2", 0), (1, 8, 0, "mix_w2", 0), (2, 32, 0, "ffn_w2", 0)])
            stat()
            apply(lambda k: gain[:, 0, k:k + 1], src=ctxx, shift=lambda k: mod[:, 0, k, 1:2], col=T)
            stat()
            dve.wait_ge(R["h_lo_done"], rounded[0])
            apply(lambda k: gain[:, 1, k:k + 1], shift=lambda k: mod[:, 0, k, 0:1])
            for d, name in ((0, "e_ff"), (1, "e_fb")):
                jobs(name, lambda n, j, b, d=d: V.tensor_copy(hf[d][:, n, :], b[:]))
            jobs("e_hi", lambda n, j, b: V.tensor_copy(hv[:, 2 * (n % 2):2 * (n % 2) + 2, 256 * (n // 2):256 * (n // 2) + 256],
                                                       pair(b[:])))
            jobs("e_hq", lambda n, j, b: V.tensor_copy(hq[:, 2 * n:2 * n + 2, :], pair(b[:])))
            jobs("e_hg", lambda n, j, b: V.tensor_copy(hg[:, 2 * n:2 * n + 2, :], pair(b[:])))
            lg = vc("hg_lb", 0, 16).rearrange("p (l d h) -> p l d h", l=2, d=2)
            step(V.tensor_tensor(lb[:, 2], lg[:, 0], lg[:, 1], ALU.max))
            sync()
            step(V.tensor_tensor(lb[:, 0], lg[:, 0], lb[:, 2], ALU.subtract))
            V.tensor_tensor(lb[:, 1], lg[:, 1], lb[:, 2], ALU.subtract).then_inc(R["lb_in"], 1)
            dve.wait_ge(R["lb_exp"], 1)
            step(V.tensor_tensor(lb[:, 3], lb[:, 0], lb[:, 1], ALU.add))
            sync()
            step(V.reciprocal(lb[:, 3], lb[:, 3]))
            sync()
            step(V.tensor_tensor(lb[:, 2], lb[:, 0], lb[:, 3], ALU.mult))
            sync()
            step(V.tensor_scalar(lb[:, 3], lb[:, 2], -1.0, 1.0, ALU.mult, ALU.add))
            step(V.memset(s_am[0], 0.0))
            step(V.memset(s_am[1], 0.0))
            sync()
            dve.wait_ge(ld["hcons"], 16)
            dve.wait_ge(R["hgf_sig"], 2 * HGH)
            dve.wait_ge(R["hgq_silu"], 4)
            chunk_mask = [cn("m_f"), cn("m_b")]
            resets = [cn("scan_f"), cn("scan_b")]

            def values(h):
                for tb in range(2):
                    for c in range(4):
                        V.tensor_scalar(s_vb[:, tb, c * P:c * P + P], hv[:, tb, h * P:h * P + P],
                                        cn("row4")[:, c:c + 1], None, ALU.mult).then_inc(R["hg_vb"], 1)

            def forget(e):
                h, d = e // 2, e % 2
                V.tensor_scalar(s_fg[d], hf[d][:, h, :], lb[:, 3, d, h:h + 1], lb[:, 2, d, h:h + 1],
                                ALU.mult, ALU.add).then_inc(R["hg_fg"], 1)

            def mask(e):
                dve.wait_ge(R["hg_att"], e + 1)
                if e >= 2:
                    dve.wait_ge(R["hg_o"], e - 1)
                V.copy_predicated(s_am[e % 2], chunk_mask[e % 2].bitcast(U32), Dn[0][:, 0:T]) \
                    .then_inc(R["hg_am"], 1)

            def decays(e):
                d = e % 2
                dve.wait_ge(R["hg_g"], e + 1)
                order = (lambda ap: ap[:, ::-1]) if d else (lambda ap: ap)
                V.tensor_tensor_scan(order(s_b[d]), order(resets[d]), order(s_b[d]), 0.0, ALU.mult, ALU.add) \
                    .then_inc(R["hg_b"], 1)
                step(V.tensor_scalar(s_fg[d], s_fg[d], -1.0, 1.0, ALU.mult, ALU.add))
                dve.wait_ge(R["hg_b"], e + 1)
                c3 = s_b[d][:, 0:T].rearrange("p (c n) -> p c n", n=CH)
                end = c3[:, :, 0:1] if d else c3[:, :, CH - 1:CH]
                cend = s_b[d][:, T:T + 1] if d else s_b[d][:, 511:512]
                step(V.tensor_tensor(s_bd[d][:, 0:T].rearrange("p (c n) -> p c n", n=CH),
                                     end.to_broadcast([P, NCH, CH]), c3, ALU.subtract))
                V.tensor_tensor(s_bd[d][:, T:512], cend.to_broadcast([P, T]), s_b[d][:, T:512], ALU.subtract) \
                    .then_inc(R["hg_bd"], 1)

            def states(e):
                chunks = list(range(NCH))[::-1] if e % 2 else list(range(NCH))
                dve.wait_ge(R["hg_u"], e + 1)
                if e:
                    dve.wait_ge(R["hg_o"], e)
                step(V.tensor_copy(s_st[:, chunks[0], :], Dn[1][:, 0:P]))
                sync()
                for a, b in zip(chunks[:-1], chunks[1:]):
                    ins = V.scalar_tensor_tensor(s_st[:, b, :], s_st[:, a, :], s_dec[e % 2][:, a:a + 1],
                                                 Dn[2 + a // 4][:, (a % 4) * P:(a % 4) * P + P], ALU.mult, ALU.add)
                    if b == chunks[-1]:
                        ins.then_inc(R["hg_st"], 1)
                    else:
                        step(ins)
                        sync()

            def decayed(e):
                h, d = e // 2, e % 2
                dve.wait_ge(R["hg_e"], 4 * e + 4)
                sync()
                step(V.tensor_tensor(s_q[d], s_q[d], hq[:, h, :], ALU.mult))
                step(V.tensor_tensor(s_k[d], s_k[d], s_fg[d][:, 0:T], ALU.mult))
                V.tensor_tensor(s_bd[d], s_bd[d], s_fg[d], ALU.mult).then_inc(R["hg_kd"], 1)

            values(0)
            passes = 2 * HGH
            for i in range(passes + 3):
                if i < passes:
                    forget(i)
                if i >= 4 and i % 2 == 0:
                    h = i // 2 - 2
                    dve.wait_ge(R["hg_rs"], h + 1)
                    step(V.scalar_tensor_tensor(hf[1][:, h, 0:T], L[h % 2][:, 0:T], vc("hg_w", h), rs[:],
                                                ALU.mult, ALU.mult))
                    sync()
                    V.tensor_tensor(hf[0][:, h, T:512], hf[1][:, h, 0:T], hg[:, h, :], ALU.mult) \
                        .then_inc(R["hg_h"], 1)
                if i < passes:
                    decays(i)
                if 0 < i <= passes:
                    mask(i - 1)
                if i >= 4 and i % 2 == 0:
                    dve.wait_ge(R["mix_hi_done"], MIX["B"] + h + 1)
                    V.tensor_tensor(mix_lo[:, 4 + h, :], hf[0][:, h, T:512], mix_hi[:, 4 + h, :].bitcast(FP),
                                    ALU.subtract).then_inc(R["mix_lo_done"], 1)
                if i >= 3 and i % 2:
                    h = (i - 3) // 2
                    dve.wait_ge(R["hg_ss"], h + 1)
                    step(V.tensor_scalar(var[:], N0[:, 0:T], 1.0 / P, EPS, ALU.mult, ALU.add))
                    sync()
                    V.reciprocal(var[:], var[:]).then_inc(R["hg_rv"], 1)
                if 0 < i <= passes:
                    states(i - 1)
                if i < passes:
                    decayed(i)
                if i and i % 2 == 0 and i < passes:
                    values(i // 2)
            past_ada("ada_h")
            modulation(1, [(3, 8, 0, "mix_w2", KB), (4, 32, 0, "ffn_w2", KB)])
            jobs("e_nq", lambda n, j, b: V.tensor_scalar(nq[:, 2 * n:2 * n + 2, :], pair(b[:]), 0.125, None, ALU.mult))
            jobs("e_nk", lambda n, j, b: V.tensor_copy(nk[:, n, :], b[:]))
            jobs("e_nv", lambda n, j, b: V.tensor_copy(nv[:, 2 * (n % 2):2 * (n % 2) + 2, 256 * (n // 2):256 * (n // 2) + 256],
                                                       pair(b[:])))
            dve.wait_ge(ld["nbias"], 16 * 16)
            V.tensor_tensor(nbias, nbias, cn("na").unsqueeze(1).to_broadcast([P, 48, 64]), ALU.add) \
                .then_inc(R["bias_ready"], 1)
            attention(T_N, len(T_A) + len(T_B), 10, MIX["hg"])
            residual("e_out", lambda k: mod[:, 0, 16 + k, 0:1])
            stat()
            apply(lambda k: gain[:, 2, k:k + 1], shift=lambda k: mod[:, 0, 24 + k, 0:1])
            ffn("ffn2", 2, CENTRED3, lambda k: mod[:, 0, 40 + k, 0:1])

            stat()
            apply(lambda k: gain[:, 3, k:k + 1], shift=lambda k: mod[:, 1, k, 0:1])
            jobs("o_b", lambda n, j, b: V.tensor_copy(ogb[:, 2 * n:2 * n + 2, :], pair(b[:])))

            def c_or_u(n, j, b):
                if n % 2 == 0:
                    return V.tensor_copy(ogc, pair(b[:]))
                return V.tensor_tensor(ocu, ogc, pair(b[:]), ALU.mult)

            def short_conv(n):
                dve.wait_ge(job_evac, JOBS["o_cu"][2 * n + 1].banked + 1)
                at = VECS["od_conv"][0] + 8 * n
                if n:
                    dve.wait_ge(R["mix_lo_done"], MIX["na"] + n)
                step(conv(ocv, ocu, [(lambda c, o=o: vec[:, at + 4 * c + o:at + 4 * c + o + 1]) for o in range(3)],
                          lambda c: vec[:, at + 4 * c + 3:at + 4 * c + 4], CENTRED3))
                sync()
                V.tensor_tensor(ocv, ocv, ogb[:, 2 * n:2 * n + 2, :], ALU.mult).then_inc(R["od_h"], 1)
                dve.wait_ge(R["mix_hi_done"], MIX["na"] + n + 1)
                V.tensor_tensor(mix_lo[:, 2 * n:2 * n + 2, :], ocv, mix_hi[:, 2 * n:2 * n + 2, :].bitcast(FP),
                                ALU.subtract).then_inc(R["mix_lo_done"], 1)

            for n, j in enumerate(JOBS["o_cu"]):
                upto(j.unit + 2)
                dve.wait_ge(job_done, j.number + 1)
                c_or_u(n, j, bank(j)).then_inc(job_evac, 1)
                dve.wait_ge(job_evac, j.banked + 1)
                if n % 2:
                    short_conv(n // 2)
            residual("o_out", lambda k: mod[:, 1, 16 + k, 0:1])
            stat()
            apply(lambda k: gain[:, 4, k:k + 1], shift=lambda k: mod[:, 1, 24 + k, 0:1])
            ffn("ffn3", 3, CENTRED3, lambda k: mod[:, 1, 40 + k, 0:1])
            stat()
            apply(lambda k: vc("fin_w2", k), to_h=False)

        @block.tensor
        def _(pe):
            mm = nc.tensor.matmul
            stats, h_in = [0], [0]

            def mm3(dst, w, h, start, stop):
                for n, (a, b) in enumerate(((0, 0), (0, 1), (1, 0))):
                    ins = mm(dst, w[a], h[b], start=start and n == 0, stop=stop and n == 2, skip_group_check=True)
                return ins

            def job(j, first=False, h_base=None, mixed=None):
                s = j.unit % RING
                w = [r[s][:].rearrange("p (k n) -> p k n", n=256) for r in (whi, wlo)]
                rows = (mix_hi, mix_lo) if j.src == "mix" else (h_hi, h_lo)
                c0, cw = {"lat": (0, T), "mix": (0, T), "ctx": (T, T), "both": (0, 512)}[j.src]
                pe.wait_ge(unit_lo, j.unit + 1)
                if j.banked >= 2:
                    pe.wait_ge(job_evac, j.banked - 1)
                b = L[j.banked % 2]
                for part in range(1 if j.kind == "fm2" else 2):
                    for k in range(KB):
                        if first and part == 0 and h_base is not None:
                            pe.wait_ge(R["h_lo_done"], h_base + k + 1)
                        if first and part == 0 and mixed is not None:
                            pe.wait_ge(R["mix_lo_done"], mixed(k))
                        if j.kind in ("fm", "ffn"):
                            dst = b[:, part * T:part * T + T]
                            W = [q[:, k, part * P:part * P + P] for q in w]
                            H = [q[:, k, c0:c0 + cw] for q in rows]
                        elif j.kind == "fm2":
                            dst = b[:]
                            W = [q[:, k, j.half * P:j.half * P + P] for q in w]
                            H = [q[:, k, :] for q in rows]
                        else:
                            dst = b[:, part * 256:part * 256 + 256]
                            at = (c0 if j.kind == "tm" else j.half * T) + part * P
                            W = [q[:, k, at:at + P] for q in rows]
                            H = [q[:, k, :] for q in w]
                        ins = mm3(dst, W, H, k == 0, k == KB - 1)
                ins.then_inc(job_done, 1)

            def jobs(name, fresh=False, after={}, mixed=None):
                for n, j in enumerate(JOBS[name]):
                    job(j, n == 0, h_in[0] if fresh else None, mixed)
                    if n == 0 and fresh:
                        h_in[0] += KB
                    if n in after:
                        after[n]()

            def turn(n):
                pe.wait_ge(R["ada_out"], 2 * n + 2)
                name = MODS[n][0]
                for c in range(2):
                    ins = mm(m_cols[:, 2 * n + c, :], ada_row[name][c], cn("fold")[0:4], start=True,
                             stop=True)
                ins.then_inc(R["ada_turned"], 1)

            def modulate(name, u):
                v, n = JOBS[name][u].unit, ADA[name] + u
                if u:
                    turn(n - 1)
                pe.wait_ge(unit_lo, v + 1)
                for k in range(KB):
                    for q in (whi, wlo):
                        ins = mm(m_rows, sc_hl[:, k, :], q[v % RING][:, k * 256:k * 256 + 256],
                                 start=k == 0 and q is whi, stop=k == KB - 1 and q is wlo)
                ins.then_inc(job_done, 1)

            def sums(i):
                pe.wait_ge(R["sq_done"], 4 * stats[0] + i + 1)
                for k in (2 * i, 2 * i + 1):
                    ins = mm(N0[:, 0:T], ones[:, 0:P], sq[:, k, :], start=k == 0, stop=k == KB - 1)
                if i == 3:
                    ins.then_inc(R["ss_done"], 1)
                    stats[0] += 1

            def stat():
                for i in range(4):
                    sums(i)

            def residual(name, mixed):
                if JOBS[name][0].banked % 2 == 0 and name != "o_out":
                    pe.wait_ge(R["mix_lo_done"], mixed(KB - 1))
                jobs(name, after={1: lambda: sums(0), 2: lambda: sums(1)}, mixed=mixed)
                sums(2)
                sums(3)

            def attention(tl, t0, g0, mixbase, ada=None):
                n = len(tl)
                for i in range(n + 3):
                    if i < n:
                        a, g = tl[i], t0 + i
                        if g >= 3:
                            pe.wait_ge(R["at_exp"], g - 2)
                        b = SB_[g % 3]
                        ins = mm(b[:, 0:a["w"]], a["q"], a["k"], start=True, stop=a["bias"] is None)
                        if a["bias"] is not None:
                            ins = mm(b[:, 0:a["nb"]], cn("flip"), a["bias"], start=False, stop=True)
                        ins.then_inc(R["at_sc"], 1)
                    if 0 <= i - 2 < n:
                        a, g = tl[i - 2], t0 + i - 2
                        pe.wait_ge(R["at_nrm"], g + 1)
                        if g >= 2:
                            pe.wait_ge(R["at_pt"], g - 1)
                        for kb in range(a["w"] // P):
                            ins = nc.tensor.transpose(PT_[g % 2][:, kb * P:kb * P + P],
                                                      a["p"][g % 3][:, kb * P:kb * P + P], ident)
                        ins.then_inc(R["at_tp"], 1)
                    if i >= 3:
                        a, g = tl[i - 3], t0 + i - 3
                        gg = (i - 3) // 4
                        pe.wait_ge(R["at_pt"], g + 1)
                        if (i - 3) % 4 == 0 and gg >= 2:
                            pe.wait_ge(R["mix_lo_done"], mixbase + gg - 1)
                        pr, c = a["pr"], a["qb"] * P
                        dst = OB[(g0 + gg) % 2][pr:pr + 64, c:c + P]
                        for kb, v in enumerate(a["v"]):
                            ins = mm(dst, v, a["t"][g % 2][:, kb * P:kb * P + P], start=kb == 0,
                                     stop=kb == len(a["v"]) - 1)
                        ins.then_inc(R["at_o"], 1)
                    if ada and i < n and i % 2 == 0:
                        modulate(ada, i // 2)
                if ada:
                    turn(23)

            def ffn(name, f):
                jl = JOBS[name]
                j0, u0, b0 = jl[0].number, jl[0].unit, jl[0].banked

                def chunk(r, i, which):
                    s = (u0 + r) % RING
                    pe.wait_ge(unit_lo, i * 3 + (u0 + r + 1))
                    pe.wait_ge(job_evac, i * 2 + (b0 + which - 1))
                    b = L[(b0 + which) % 2]
                    w = [q[s][:].rearrange("p (k n) -> p k n", n=256) for q in (whi, wlo)]
                    for part in range(2):
                        for k in range(KB):
                            ins = mm3(b[:, part * T:part * T + T], [q[:, k, part * P:part * P + P] for q in w],
                                      [q[:, k, 0:T] for q in (h_hi, h_lo)], k == 0, k == KB - 1)
                    ins.then_inc(job_done, 1)

                def down(r, i, first=False):
                    s = (u0 + r) % RING
                    pe.wait_ge(unit_lo, i * 3 + (u0 + r + 1))
                    pe.wait_ge(R["hdl_done"], i + f * NI)
                    w = [q[s][:].rearrange("p (k n) -> p k n", n=D) for q in (whi, wlo)]
                    for kt in range(2):
                        for c in range(KB):
                            ins = mm3(Dn[c // 2][:, (c % 2) * T:(c % 2) * T + T],
                                      [q[:, kt, c * P:c * P + P] for q in w],
                                      [q[:, kt, :] for q in (hd_hi, hd_lo)],
                                      first and kt == 0 and c % 2 == 0, False)
                    ins.then_inc(job_done, 1)

                def last_down():
                    s = (u0 + 3 * NI - 1) % RING
                    pe.wait_ge(unit_lo, u0 + 3 * NI)
                    pe.wait_ge(R["hdl_done"], NI * (f + 1))
                    w = [q[s][:].rearrange("p (k n) -> p k n", n=D) for q in (whi, wlo)]
                    for c in range(KB):
                        for kt in range(2):
                            ins = mm3(Dn[c // 2][:, (c % 2) * T:(c % 2) * T + T],
                                      [q[:, kt, c * P:c * P + P] for q in w],
                                      [q[:, kt, :] for q in (hd_hi, hd_lo)], False, kt == 1)
                        if c % 2 and c < KB - 1:
                            ins.then_inc(R["down_done"], 1)
                    ins.then_inc(job_done, 1)

                job(jl[0], True, h_in[0])
                h_in[0] += KB
                for j in jl[1:4]:
                    job(j)
                down(1, 1, first=True)
                with pe.Fori(2, NI - 1) as i:
                    chunk(-1, i, 0)
                    chunk(0, i, 1)
                    down(1, i)
                i = NI - 1
                chunk(-1, i, 0)
                chunk(0, i, 1)
                down(1, i)
                last_down()
                stat()

            pe.wait_ge(R["ctx_lo"], 1)
            jobs("mk0")
            pe.wait_ge(R["ones_set"], 1)
            stat()
            for name in ("mv0", "mk1", "mv1"):
                jobs(name)

            def gate_products():
                pe.wait_ge(ld["gate"], 16)
                for tb in range(2):
                    for k in range(KB):
                        ins = mm(N0[:, 8 * tb:8 * tb + 8], t[:, k, tb * P:tb * P + P], gw[:, k, :],
                                 start=k == 0, stop=k == KB - 1)
                ins.then_inc(R["gate_tm"], 1)

            def gate_transposes():
                pe.wait_ge(ld["con"], 16)
                pe.wait_ge(R["gate_sum"], 1)
                for which in range(2):
                    for tb in range(2):
                        ins = nc.tensor.transpose(N0[0:4, which * T + tb * P:which * T + tb * P + P],
                                                  g_tm[:, tb, 4 * which:4 * which + 4], ident)
                ins.then_inc(R["gate_T"], 1)

            jobs("a_qk", fresh=True, after={0: gate_products, 2: gate_transposes})
            jobs("a_v")
            pe.wait_ge(R["row_ready"], 1)
            for tb in range(2):
                ins = nc.tensor.transpose(N0[:, 4 * tb:4 * tb + 4], g_row[0:4, 0, tb * P:tb * P + P],
                                          ident[0:4, 0:4])
            ins.then_inc(R["acol_T"], 1)
            jobs("a_o")
            jobs("a_qm")

            def scores(h):
                full, half, pr = pieces(h)
                hp = slice(pr, pr + 64)
                sel = m_sel[0:4, h, :]
                mm(Dn[1][:, 0:T], sel, g_row[0:4, 4, :], start=True, stop=True)
                mm(Dn[1][:, T:512], sel, g_row[0:4, 5, :], start=True, stop=True)
                for sb_, (c, w) in enumerate(((0, T), (T, P))):
                    q0 = T - w
                    mm(Dn[0][:, c:c + w], ak[:, full, sb_ * P:sb_ * P + P], aq[:, full, q0:T],
                       start=True, stop=False)
                    ins = mm(Dn[0][:, c:c + w], ak[hp, half, sb_ * P:sb_ * P + P], aq[hp, half, q0:T],
                             start=False, stop=True)
                ins.then_inc(R["ml_s"], 1)

            def weighted(dst, lhs):
                mm(dst, lhs(0), m_p[:, 0:T], start=True, stop=False)
                return mm(dst[:, P:T], lhs(1), m_p[:, T:T + P], start=False, stop=True)

            pe.wait_ge(R["em_ready"], 1)
            pe.wait_ge(R["q_silu"], 6)
            pe.wait_ge(R["sc_lo"], 1)
            scores(0)
            for h in range(MH):
                full, half, pr = pieces(h)
                hp = slice(pr, pr + 64)
                pe.wait_ge(R["ml_p"], h + 1)
                if h + 1 < MH:
                    scores(h + 1)
                if h:
                    pe.wait_ge(R["ml_post"], h)
                weighted(Dn[2][:, 0:T], lambda s: av[:, s, full * P:full * P + P])
                weighted(Dn[2][hp, T:512], lambda s: av[:, s, half * P + pr:half * P + pr + 64])
                weighted(Dn[3][:, 0:T], lambda s: ones[:, 0:P]).then_inc(R["ml_num"], 1)
                pe.wait_ge(R["ml_sq"], 2 * h + 2)
                mm(N0[:, 0:T], ones[:, 0:P], m_sq[:, 0, :], start=True, stop=False)
                mm(N0[:, 0:T], ones[hp, 0:P], m_sq[hp, 1, :], start=False, stop=True).then_inc(R["ml_ss"], 1)
                modulate("ada_a", 2 * h)
                modulate("ada_a", 2 * h + 1)
            turn(7)
            pe.wait_ge(R["mix_lo_done"], MIX["ml"])
            pe.wait_ge(job_evac, evacuated("a_out"))
            attention(T_A, 0, 0, MIX["ml"])
            residual("a_out", lambda k: MIX["ml"] + max(k - 5, 0))
            ffn("ffn0", 0)

            jobs("kv_k", fresh=True)
            jobs("kv_v")
            jobs("b_q", fresh=True)
            jobs("b_qm")
            pe.wait_ge(job_evac, evacuated("b_out"))
            pe.wait_ge(R["bias_ready"], 2)
            attention(T_B, len(T_A), 2, MIX["memA"], "ada_b")
            residual("b_out", lambda k: MIX["memA"] + k + 1)
            ffn("ffn1", 1)

            stat()
            stat()
            h_in[0] += KB
            pe.wait_ge(R["mod_ready"], 1)
            jobs("e_ff", fresh=True)
            jobs("e_fb")
            jobs("e_hi")
            jobs("e_hq")
            jobs("e_hg")
            pe.wait_ge(job_evac, evacuated("e_nq"))

            def head_sums(h):
                pe.wait_ge(R["hg_sq"], h + 1)
                mm(N0[:, 0:T], ones[:, 0:P], hf[0][:, h, 0:T], start=True, stop=True).then_inc(R["hg_ss"], 1)

            for e in range(2 * HGH):
                h, d = e // 2, e % 2
                pe.wait_ge(R["hg_kd"], e + 1)
                for tb in range(2):
                    mm(Dn[0][:, tb * P:tb * P + P], s_k[d][:, tb * P:tb * P + P], s_q[d][:, tb * P:tb * P + P],
                       start=True, stop=True)
                for b in range(4):
                    ins = nc.tensor.transpose(Dn[1][:, b * P:b * P + P], s_bd[d][:, b * P:b * P + P], ident)
                ins.then_inc(R["hg_att"], 1)
                modulate("ada_h", 3 * e)
                if d == 0 and h:
                    head_sums(h - 1)
                pe.wait_ge(R["hg_kdt"], e + 1)
                if d == 0:
                    pe.wait_ge(R["hg_vb"], 8 * h + 8)
                for tb in range(2):
                    mm(Dn[1][:, 0:P], s_kt[:, 2 + tb, :], hv[:, 2 + tb, h * P:h * P + P], start=tb == 0,
                       stop=tb == 1)
                for tb in range(2):
                    ins = mm(Dn[2 + tb][:], s_kt[:, tb, :], s_vb[:, tb, :], start=True, stop=True)
                ins.then_inc(R["hg_u"], 1)
                modulate("ada_h", 3 * e + 1)
                pe.wait_ge(R["hg_am"], e + 1)
                pe.wait_ge(R["hg_st"], e + 1)
                if d == 0 and h >= 2:
                    pe.wait_ge(R["hg_h"], h - 1)
                for tb in range(2):
                    mm(L[h % 2][:, tb * P:tb * P + P], hv[:, tb, h * P:h * P + P], s_am[d][:, tb * P:tb * P + P],
                       start=d == 0 and tb == 0, stop=False, skip_group_check=True)
                for c in range(NCH):
                    ins = mm(L[h % 2][:, c * CH:c * CH + CH], s_st[:, c, :], s_q[d][:, c * CH:c * CH + CH],
                             start=False, stop=d == 1 and c == NCH - 1, skip_group_check=True)
                ins.then_inc(R["hg_o"], 1)
                modulate("ada_h", 3 * e + 2)
            head_sums(HGH - 1)
            turn(47)
            pe.wait_ge(R["mix_lo_done"], MIX["hg"])
            jobs("e_nq")
            jobs("e_nk")
            jobs("e_nv")
            pe.wait_ge(job_evac, evacuated("e_out"))
            pe.wait_ge(R["bias_ready"], 3)
            attention(T_N, len(T_A) + len(T_B), 10, MIX["hg"])
            residual("e_out", lambda k: MIX["hg"] + min(k + 1, 4))
            ffn("ffn2", 2)

            jobs("o_b", fresh=True)
            jobs("o_cu")
            residual("o_out", lambda k: MIX["na"] + k // 2 + 1)
            ffn("ffn3", 3)


def kernel(**inputs):
    import numpy as np
    import concourse.bacc as bacc
    from concourse.bass_utils import run_bass_kernel_spmd as run

    a = {k: np.asarray(v) for k, v in inputs.items()}

    def rows(m):
        return np.ascontiguousarray(m.T.reshape(KB, P, -1).transpose(1, 0, 2))

    def cols(v):
        v = v.reshape(v.shape[:-1] + (-1, P))
        return np.moveaxis(v, -1, 0)

    def units(w):
        n = w.shape[1] // 256
        return w.reshape(KB, P, n, 256).transpose(2, 1, 0, 3).reshape(n, P, 2048)

    def ffn_units(first, second, down):
        g, u = units(first), units(second)
        d = down.reshape(NI, 2, P, D).transpose(0, 2, 1, 3).reshape(NI, P, 2048)
        out = [g[0], u[0]]
        for i in range(1, NI):
            out += [g[i], u[i], d[i - 1]]
        return np.stack(out + [d[NI - 1]])

    wa, e, o = a["a_w_in"][0], a["ev_w_in_2"][0], a["od_w_in_2"][0]
    ev = [units(e[:, 512 * i:512 * i + 512]) for i in range(8)]
    oc, ou = units(o[:, D:2 * D]), units(o[:, 2 * D:])
    mem_kv = [units(a["mem_w_kv"][l]) for l in range(2)]
    ada = [units(a["ada_w_2"][l]) for l in range(2)]
    up, up2 = a["ffn_w_up"], a["ffn_w_up_2"]
    stream = [
        mem_kv[0], mem_kv[1],
        units(wa[:, :3072]), units(wa[:, 3080:]), ada[0][:8], units(a["a_w_out"][0]),
        ffn_units(up[0][:, FF:], up[0][:, :FF], a["ffn_w_down"][0]),
        units(a["w_kv"]), units(a["b_w_in"][0]), ada[0][8:], units(a["b_w_out"][0]),
        ffn_units(up[1][:, FF:], up[1][:, :FF], a["ffn_w_down"][1]),
        ev[4], ev[5], ev[6], ev[3], ev[7], ada[1], ev[0], ev[1], ev[2], units(a["ev_w_out_2"][0]),
        ffn_units(up2[0][:, :FF], up2[0][:, FF:], a["ffn_w_down_2"][0]),
        units(o[:, :D]), np.stack([oc, ou], 1).reshape(8, P, 2048), units(a["od_w_out_2"][0]),
        ffn_units(up2[1][:, :FF], up2[1][:, FF:], a["ffn_w_down_2"][1]),
    ]

    def taps(w, b, order):
        return np.concatenate([cols(w[list(order)]).transpose(0, 2, 1), cols(b)[:, :, None]], axis=2)

    CAUSAL, CENTRED = (2, 1, 0), (1, 0, 2)
    ffn_taps = [taps(a["ffn_conv_w"][l], a["ffn_conv_b"][l], CAUSAL) for l in range(2)] + \
               [taps(a["ffn_conv_w_2"][l], a["ffn_conv_b_2"][l], CENTRED) for l in range(2)]
    parts = {
        "mix_g": cols(a["norm_mix_g"]), "ffn_g": cols(a["norm_ffn_g"]), "kv_g": cols(a["kv_norm_g"]),
        "fin_g": cols(a["final_g"]), "mix_w2": cols(a["norm_mix_w_2"]), "ffn_w2": cols(a["norm_ffn_w_2"]),
        "fin_w2": cols(a["final_norm_w_2"]),
        "a_conv": taps(a["a_conv_w"][0], a["a_conv_b"][0], (3, 2, 1, 0)),
        "a_head": cols(a["a_head_g"][0]),
        "ffn_conv": np.stack(ffn_taps, 1),
        "od_conv": taps(a["od_conv_w_2"][0], a["od_conv_b_2"][0], CENTRED),
        "ada_b": cols(a["ada_b_2"]), "hg_lb": cols(a["hg_lb_logits_2"]), "hg_w": cols(a["hg_norm_w_2"][0]),
        "cc": cols(np.stack([a["c_2"][0], a["c_ctx_2"]])).transpose(0, 2, 1),
        "gate_b": np.broadcast_to(a["a_gate_b"][0], (P, 8)),
    }
    vecs = np.concatenate([parts[n].reshape(P, -1) for n in VECS], axis=1)

    i = np.arange(P)
    q, k = i[:, None], i[None, :]
    same = (q // CH) == (k // CH)
    f32 = np.float32
    scan_f, scan_b = np.ones((P, 512), f32), np.ones((P, 512), f32)
    scan_f[:, 0:T:CH] = 0
    scan_f[:, T] = 0
    scan_b[:, CH - 1:T:CH] = 0
    scan_b[:, 511] = 0
    c = i % 64
    start = np.clip(c - 8, 0, 48)[:, None]
    cc = np.arange(64)[None, :]
    consts = {
        "ident": np.eye(P, dtype=f32), "flip": np.eye(P, dtype=f32)[::-1], "causal": (q <= k).astype(f32),
        "m_f": np.tile((same & (q <= k)).astype(f32), (1, 2)), "m_b": np.tile((same & (q >= k)).astype(f32), (1, 2)),
        "scan_f": scan_f, "scan_b": scan_b, "row4": (i[:, None] // CH == np.arange(4)[None]).astype(f32),
        "fold": (np.minimum(i, 4)[:, None] % 2 == np.arange(2)[None]).astype(f32) * (i[:, None] < 4),
        "na": np.where((cc >= start) & (cc < start + 16), 0, NEG).astype(f32)[::-1],
    }
    cons = np.concatenate([consts[n] for n in CONS], axis=1)
    hcons = np.concatenate([consts[n] for n in HCONS], axis=1)

    relx = np.pad(a["b_rel_bias"][0][:, ::-1], ((0, 0), (127, 193)), mode="edge")
    nax = np.pad(a["na_rpb_2"][0][:, 4:11, :], ((0, 0), (0, 0), (48, 48)))

    arrays = {
        "x": rows(a["x"][0]), "mem": rows(a["mem"][0]), "ctx": rows(a["ctx_2"][0]),
        "vecs": vecs, "cons": cons, "gate": wa[:, 3072:3080].reshape(KB, P, 8).transpose(1, 0, 2),
        "units": np.concatenate(stream), "hcons": hcons, "relx": relx, "nax": nax,
    }
    nc = bacc.Bacc("TRN2", target_bir_lowering=False, num_devices=1)
    io = {}
    for n in arrays:
        arrays[n] = np.ascontiguousarray(arrays[n])
        io[n] = nc.dram_tensor(f"in_{n}", arrays[n].shape, FP, kind="ExternalInput").ap()
    out = nc.dram_tensor("out_0", (P, KB, T), FP, kind="ExternalOutput").ap()
    build(nc, io, out)
    r = run(nc, [{f"in_{n}": v for n, v in arrays.items()}], core_ids=[0])
    got = r.results[0]["out_0"]
    return got.transpose(2, 1, 0).reshape(1, T, D)
```
